# Optimizing a Trainium2 kernel written in Bass

```python
import math
import jax, jax.numpy as jnp
from jax import lax
import numpy as np

D_MODEL = 2048
BATCH = 1
SEQ = 256
DEPTH = 1

N_META = 16
GDN_HEADS = 16
GDN_DK = 128
GDN_DV = 128
CONV_K = 4
CHUNK = 64
FOX_HEADS = 16
FOX_DH = 128
Q_BLOCK = 128
D_FF = 4 * D_MODEL
NORM_EPS = 1e-6

GDN_QK = GDN_HEADS * GDN_DK
GDN_V = GDN_HEADS * GDN_DV
GDN_CONV_DIM = 2 * GDN_QK + GDN_V
FOX_W = FOX_HEADS * FOX_DH
IN_SPLITS = (GDN_CONV_DIM, GDN_V, GDN_HEADS, GDN_HEADS, 3 * FOX_W, FOX_HEADS, D_MODEL, D_MODEL)
N_IN = sum(IN_SPLITS)
IN_SPLIT_IDX = tuple(int(i) for i in np.cumsum(IN_SPLITS)[:-1])


def rms_norm(x, g):
    xf = x.astype(jnp.float32)
    y = xf * lax.rsqrt(jnp.mean(jnp.square(xf), axis=-1, keepdims=True) + NORM_EPS)
    return (y * g.astype(jnp.float32)).astype(x.dtype)

def l2_normalize(x):
    return x * lax.rsqrt(jnp.sum(jnp.square(x), axis=-1, keepdims=True) + NORM_EPS)

def causal_depthwise_conv(x, w):
    L = x.shape[1]
    xp = jnp.pad(x, ((0, 0), (CONV_K - 1, 0), (0, 0)))
    return sum(xp[:, k:k + L] * w[k] for k in range(CONV_K))

def chunked_gated_delta_rule(q, k, v, g, beta):
    B, H, L, DK = q.shape
    DV = v.shape[-1]
    N = L // CHUNK
    rs = lambda t: t.reshape(B, H, N, CHUNK, *t.shape[3:])
    q, k, v, g, beta = rs(q) * DK ** -0.5, rs(k), rs(v), rs(g), rs(beta)
    g = jnp.cumsum(g, axis=-1)
    causal = jnp.tril(jnp.ones((CHUNK, CHUNK), bool))
    strict = jnp.tril(jnp.ones((CHUNK, CHUNK), bool), -1)
    decay = jnp.exp(jnp.where(causal, g[..., :, None] - g[..., None, :], -jnp.inf))
    k_beta = k * beta[..., None]
    a_mat = jnp.where(strict, jnp.einsum('bhncd,bhnsd->bhncs', k_beta, k) * decay, 0.0)
    eye = jnp.eye(CHUNK, dtype=q.dtype)
    rhs = jnp.concatenate([v * beta[..., None], k_beta * jnp.exp(g)[..., None]], axis=-1)
    sol = lax.linalg.triangular_solve(a_mat + eye, rhs, left_side=True, lower=True, unit_diagonal=True)
    w_val, w_key = sol[..., :DV], sol[..., DV:]
    qk_intra = jnp.where(causal, jnp.einsum('bhncd,bhnsd->bhncs', q, k) * decay, 0.0)
    q_dec = q * jnp.exp(g)[..., None]
    k_dec = k * jnp.exp(g[..., -1:] - g)[..., None]
    g_last = jnp.exp(g[..., -1])

    def step(S, inp):
        qk_c, q_dec_c, k_dec_c, w_val_c, w_key_c, g_last_c = inp
        v_new = w_val_c - jnp.einsum('bhck,bhkv->bhcv', w_key_c, S)
        o = jnp.einsum('bhck,bhkv->bhcv', q_dec_c, S) + jnp.einsum('bhcs,bhsv->bhcv', qk_c, v_new)
        S = S * g_last_c[..., None, None] + jnp.einsum('bhck,bhcv->bhkv', k_dec_c, v_new)
        return S, o

    xs = tuple(jnp.moveaxis(t, 2, 0) for t in (qk_intra, q_dec, k_dec, w_val, w_key, g_last))
    S0 = jnp.zeros((B, H, DK, DV), q.dtype)
    _, o = lax.scan(step, S0, xs)
    return jnp.moveaxis(o, 0, 2).reshape(B, H, L, DV)

def gated_deltanet_branch(qkv, z, b, a, conv_w, a_log, dt_bias, norm_g):
    B, L, _ = qkv.shape
    out_dtype = qkv.dtype
    f32 = jnp.float32
    pad = (-L) % CHUNK
    Lp = L + pad
    front = lambda t: jnp.pad(t, ((0, 0), (pad, 0)) + ((0, 0),) * (t.ndim - 2))
    qkv = jax.nn.silu(causal_depthwise_conv(front(qkv.astype(f32)), conv_w.astype(f32)))
    q, k, v = jnp.split(qkv, [GDN_QK, 2 * GDN_QK], axis=-1)
    q = l2_normalize(q.reshape(B, Lp, GDN_HEADS, GDN_DK))
    k = l2_normalize(k.reshape(B, Lp, GDN_HEADS, GDN_DK))
    v = v.reshape(B, Lp, GDN_HEADS, GDN_DV)
    beta = front(jax.nn.sigmoid(b.astype(f32)))
    g = front(-jnp.exp(a_log.astype(f32)) * jax.nn.softplus(a.astype(f32) + dt_bias.astype(f32)))
    bhl = lambda t: jnp.moveaxis(t, 2, 1)
    o = chunked_gated_delta_rule(bhl(q), bhl(k), bhl(v), bhl(g), bhl(beta))
    o = jnp.moveaxis(o, 1, 2)[:, pad:]
    o = rms_norm(o, norm_g) * jax.nn.silu(z.astype(f32).reshape(B, L, GDN_HEADS, GDN_DV))
    return o.reshape(B, L, GDN_V).astype(out_dtype)

def fox_branch(qkv, f_logit, q_norm_g, k_norm_g, f_bias):
    B, L, _ = qkv.shape
    pad = (-L) % Q_BLOCK
    Lp = L + pad
    nblk = Lp // Q_BLOCK
    q, k, v = jnp.split(qkv, 3, axis=-1)
    heads = lambda t: jnp.pad(t, ((0, 0), (0, pad), (0, 0), (0, 0))).transpose(0, 2, 1, 3)
    q = heads(rms_norm(q.reshape(B, L, FOX_HEADS, FOX_DH), q_norm_g))
    k = heads(rms_norm(k.reshape(B, L, FOX_HEADS, FOX_DH), k_norm_g))
    v = heads(v.reshape(B, L, FOX_HEADS, FOX_DH))
    log_f = jax.nn.log_sigmoid(f_logit.astype(jnp.float32) + f_bias.astype(jnp.float32))
    c = jnp.cumsum(log_f, axis=1)
    c = jnp.pad(c, ((0, 0), (0, pad), (0, 0)), mode='edge').transpose(0, 2, 1)
    kpos = jnp.arange(Lp)
    scale = FOX_DH ** -0.5

    def block(i):
        start = i * Q_BLOCK
        qs = lax.dynamic_slice_in_dim(q, start, Q_BLOCK, axis=2)
        cq = lax.dynamic_slice_in_dim(c, start, Q_BLOCK, axis=2)
        s = jnp.einsum('bhqd,bhkd->bhqk', qs, k).astype(jnp.float32) * scale
        s = s + cq[..., :, None] - c[..., None, :]
        qpos = start + jnp.arange(Q_BLOCK)
        s = jnp.where(kpos[None, :] <= qpos[:, None], s, -jnp.inf)
        p = jax.nn.softmax(s, axis=-1).astype(v.dtype)
        return jnp.einsum('bhqk,bhkd->bhqd', p, v)

    o = lax.map(block, jnp.arange(nblk))
    o = jnp.transpose(o, (1, 0, 3, 2, 4)).reshape(B, Lp, FOX_W)
    return o[:, :L]

def hybrid_layer(h, mix_norm_g, w_in, conv_w, a_log, dt_bias, gdn_norm_g, w_o_gdn,
                 fox_q_norm_g, fox_k_norm_g, fox_f_bias, w_o_fox, w_out, mlp_norm_g, w_up, w_down):
    u = rms_norm(h, mix_norm_g)
    p = u @ w_in
    qkv_a, z_a, b_a, a_a, qkv_b, f_b, gate_a, gate_b = jnp.split(p, IN_SPLIT_IDX, axis=-1)
    y_a = gated_deltanet_branch(qkv_a, z_a, b_a, a_a, conv_w, a_log, dt_bias, gdn_norm_g)
    y_b = fox_branch(qkv_b, f_b, fox_q_norm_g, fox_k_norm_g, fox_f_bias)
    mix = jax.nn.sigmoid(gate_a) * (y_a @ w_o_gdn) + jax.nn.sigmoid(gate_b) * (y_b @ w_o_fox)
    h = h + mix @ w_out
    u = rms_norm(h, mlp_norm_g)
    h = h + jnp.square(jax.nn.relu(u @ w_up)) @ w_down
    return h

def first_inputs(seed: int = 0) -> dict:
    key = jax.random.key(seed)
    ks = jax.random.split(key, 20)
    f32 = jnp.float32
    nrm = lambda k, shape, scale: jax.random.normal(k, shape, f32) * scale
    gain = lambda k, shape: 1.0 + 0.02 * jax.random.normal(k, shape, f32)
    x = nrm(ks[0], (BATCH, SEQ, D_MODEL), 1.0)
    meta_tokens = nrm(ks[1], (N_META, D_MODEL), 1.0)
    mix_norm_g = gain(ks[2], (DEPTH, D_MODEL))
    w_in = nrm(ks[3], (DEPTH, D_MODEL, N_IN), D_MODEL ** -0.5)
    conv_w = nrm(ks[4], (DEPTH, CONV_K, GDN_CONV_DIM), CONV_K ** -0.5)
    a_log = jnp.log(jax.random.uniform(ks[5], (DEPTH, GDN_HEADS), f32, 1.0, 16.0))
    dt = jnp.exp(jax.random.uniform(ks[6], (DEPTH, GDN_HEADS), f32, math.log(1e-3), math.log(1e-1)))
    dt_bias = dt + jnp.log(-jnp.expm1(-dt))
    gdn_norm_g = gain(ks[7], (DEPTH, GDN_DV))
    w_o_gdn = nrm(ks[8], (DEPTH, GDN_V, D_MODEL), GDN_V ** -0.5)
    fox_q_norm_g = gain(ks[9], (DEPTH, FOX_DH))
    fox_k_norm_g = gain(ks[10], (DEPTH, FOX_DH))
    fox_f_bias = jax.random.uniform(ks[11], (DEPTH, FOX_HEADS), f32, 3.0, 6.0)
    w_o_fox = nrm(ks[12], (DEPTH, FOX_W, D_MODEL), FOX_W ** -0.5)
    w_out = nrm(ks[13], (DEPTH, D_MODEL, D_MODEL), D_MODEL ** -0.5)
    mlp_norm_g = gain(ks[14], (DEPTH, D_MODEL))
    w_up = nrm(ks[15], (DEPTH, D_MODEL, D_FF), D_MODEL ** -0.5)
    w_down = nrm(ks[16], (DEPTH, D_FF, D_MODEL), D_FF ** -0.5)
    final_norm_g = gain(ks[17], (D_MODEL,))
    return {"x": x, "meta_tokens": meta_tokens, "mix_norm_g": mix_norm_g, "w_in": w_in,
            "conv_w": conv_w, "a_log": a_log, "dt_bias": dt_bias, "gdn_norm_g": gdn_norm_g,
            "w_o_gdn": w_o_gdn, "fox_q_norm_g": fox_q_norm_g, "fox_k_norm_g": fox_k_norm_g,
            "fox_f_bias": fox_f_bias, "w_o_fox": w_o_fox, "w_out": w_out, "mlp_norm_g": mlp_norm_g,
            "w_up": w_up, "w_down": w_down, "final_norm_g": final_norm_g}

def first_block(x, meta_tokens, mix_norm_g, w_in, conv_w, a_log, dt_bias, gdn_norm_g, w_o_gdn,
              fox_q_norm_g, fox_k_norm_g, fox_f_bias, w_o_fox, w_out, mlp_norm_g, w_up, w_down,
              final_norm_g):
    B = x.shape[0]
    meta = jnp.broadcast_to(meta_tokens[None].astype(x.dtype), (B, N_META, D_MODEL))
    h = jnp.concatenate([meta, x], axis=1)
    for l in range(DEPTH):
        h = hybrid_layer(h, mix_norm_g[l], w_in[l], conv_w[l], a_log[l], dt_bias[l], gdn_norm_g[l],
                         w_o_gdn[l], fox_q_norm_g[l], fox_k_norm_g[l], fox_f_bias[l], w_o_fox[l],
                         w_out[l], mlp_norm_g[l], w_up[l], w_down[l])
    return rms_norm(h, final_norm_g)[:, N_META:]


DEPTH_2 = 2

N_MIXERS = 2
ROPE_THETA = 500000.0
BLOCK = 128
POS_OFFSET_MAX = 1024
NEG_INF = -1e30

MLA_HEADS = 16
MLA_Q_RANK = 512
MLA_KV_RANK = 512
MLA_NOPE = 128
MLA_ROPE = 64
MLA_V = 128
MLA_WIDTH = MLA_HEADS * MLA_V
MLA_IN = MLA_Q_RANK + MLA_KV_RANK + MLA_ROPE + MLA_WIDTH

SWA_Q_HEADS = 32
SWA_KV_HEADS = 4
SWA_GROUP = SWA_Q_HEADS // SWA_KV_HEADS
SWA_HEAD_DIM = 64
SWA_WINDOW = 128
SWA_ROPE_DIM = SWA_HEAD_DIM // 4
SWA_WIDTH = SWA_Q_HEADS * SWA_HEAD_DIM
SWA_KV_WIDTH = SWA_KV_HEADS * SWA_HEAD_DIM
SWA_IN = SWA_WIDTH + 2 * SWA_KV_WIDTH + SWA_WIDTH

N_MLA = (DEPTH_2 + 1) // 2
N_SWA = DEPTH_2 // 2


def rmsnorm(x, g):
    xf = x.astype(jnp.float32)
    y = xf * lax.rsqrt(jnp.mean(xf * xf, axis=-1, keepdims=True) + NORM_EPS)
    return (y * g.astype(jnp.float32)).astype(x.dtype)

def rope(x, positions, rot_dim):
    half = rot_dim // 2
    inv_freq = ROPE_THETA ** (-jnp.arange(0, rot_dim, 2, dtype=jnp.float32) / rot_dim)
    ang = positions.astype(jnp.float32)[..., None] * inv_freq
    cos = jnp.cos(ang)[:, :, None, :]
    sin = jnp.sin(ang)[:, :, None, :]
    xf = x.astype(jnp.float32)
    x1, x2, rest = xf[..., :half], xf[..., half:rot_dim], xf[..., rot_dim:]
    out = jnp.concatenate([x1 * cos - x2 * sin, x2 * cos + x1 * sin, rest], axis=-1)
    return out.astype(x.dtype)

def mla_causal_attention(q_nope, q_rope, k_nope, k_rope, v):
    B, S, H, _ = q_nope.shape
    nb = S // BLOCK
    scale = (MLA_NOPE + MLA_ROPE) ** -0.5
    key_idx = jnp.arange(S)

    def one_block(i):
        start = i * BLOCK
        qn = lax.dynamic_slice_in_dim(q_nope, start, BLOCK, axis=1)
        qr = lax.dynamic_slice_in_dim(q_rope, start, BLOCK, axis=1)
        s = (jnp.einsum('bqhd,bkhd->bhqk', qn, k_nope)
             + jnp.einsum('bqhr,bkr->bhqk', qr, k_rope)).astype(jnp.float32) * scale
        q_idx = start + jnp.arange(BLOCK)
        causal = key_idx[None, :] <= q_idx[:, None]
        s = jnp.where(causal, s, NEG_INF)
        p = jax.nn.softmax(s, axis=-1).astype(v.dtype)
        return jnp.einsum('bhqk,bkhd->bqhd', p, v)

    out = lax.map(one_block, jnp.arange(nb))
    return out.transpose(1, 0, 2, 3, 4).reshape(B, S, H * MLA_V)

def mla_mixer(h, positions, w_in, q_norm, w_uq, kv_norm, w_ukv):
    B, S, _ = h.shape
    proj = h @ w_in
    c_q, c_kv, k_rope, gate = jnp.split(
        proj, [MLA_Q_RANK, MLA_Q_RANK + MLA_KV_RANK, MLA_Q_RANK + MLA_KV_RANK + MLA_ROPE], axis=-1)
    q = (rmsnorm(c_q, q_norm) @ w_uq).reshape(B, S, MLA_HEADS, MLA_NOPE + MLA_ROPE)
    q_nope = q[..., :MLA_NOPE]
    q_rope = rope(q[..., MLA_NOPE:], positions, MLA_ROPE)
    kv = (rmsnorm(c_kv, kv_norm) @ w_ukv).reshape(B, S, MLA_HEADS, MLA_NOPE + MLA_V)
    k_nope, v = kv[..., :MLA_NOPE], kv[..., MLA_NOPE:]
    k_rope = rope(k_rope[:, :, None, :], positions, MLA_ROPE)[:, :, 0, :]
    y = mla_causal_attention(q_nope, q_rope, k_nope, k_rope, v)
    return y, gate

def swa_sink_attention(q, k, v, sinks):
    B, S, _, D = q.shape
    nb = S // BLOCK
    qb = q.reshape(B, nb, BLOCK, SWA_KV_HEADS, SWA_GROUP, D)

    def band(t):
        tb = t.reshape(B, nb, BLOCK, SWA_KV_HEADS, D)
        prev = jnp.concatenate([jnp.zeros_like(tb[:, :1]), tb[:, :-1]], axis=1)
        return jnp.concatenate([prev, tb], axis=2)

    kw, vw = band(k), band(v)
    s = jnp.einsum('bnqhgd,bnkhd->bnhgqk', qb, kw).astype(jnp.float32) * (D ** -0.5)
    blk = jnp.arange(nb)[:, None, None]
    qi = jnp.arange(BLOCK)[None, :, None]
    kk = jnp.arange(2 * BLOCK)[None, None, :]
    diff = qi + BLOCK - kk
    key_abs = blk * BLOCK - BLOCK + kk
    valid = (diff >= 0) & (diff < SWA_WINDOW) & (key_abs >= 0)
    s = jnp.where(valid[None, :, None, None], s, NEG_INF)
    sink = sinks.astype(jnp.float32).reshape(1, 1, SWA_KV_HEADS, SWA_GROUP, 1, 1)
    m = jnp.maximum(jnp.max(s, axis=-1, keepdims=True), sink)
    e = jnp.exp(s - m)
    p = e / (jnp.sum(e, axis=-1, keepdims=True) + jnp.exp(sink - m))
    o = jnp.einsum('bnhgqk,bnkhd->bnqhgd', p.astype(v.dtype), vw)
    return o.reshape(B, S, SWA_WIDTH)

def swa_mixer(h, positions, w_in, sinks):
    B, S, _ = h.shape
    proj = h @ w_in
    q, k, v, gate = jnp.split(
        proj, [SWA_WIDTH, SWA_WIDTH + SWA_KV_WIDTH, SWA_WIDTH + 2 * SWA_KV_WIDTH], axis=-1)
    q = rope(q.reshape(B, S, SWA_Q_HEADS, SWA_HEAD_DIM), positions, SWA_ROPE_DIM)
    k = rope(k.reshape(B, S, SWA_KV_HEADS, SWA_HEAD_DIM), positions, SWA_ROPE_DIM)
    v = v.reshape(B, S, SWA_KV_HEADS, SWA_HEAD_DIM)
    y = swa_sink_attention(q, k, v, sinks)
    return y, gate

def second_inputs(seed: int = 0) -> dict:
    key = jax.random.key(seed)
    ks = jax.random.split(key, 16)
    f32 = jnp.float32

    def nrm(k, shape, fan_in):
        return jax.random.normal(k, shape, f32) * fan_in ** -0.5

    def gain(k, shape):
        return 1.0 + 0.05 * jax.random.normal(k, shape, f32)

    x = jax.random.normal(ks[0], (BATCH, SEQ, D_MODEL), f32)
    offset = jax.random.randint(ks[1], (BATCH, 1), 0, POS_OFFSET_MAX, dtype=jnp.int32)
    positions = offset + jnp.arange(SEQ, dtype=jnp.int32)[None, :]
    return {
        "x": x,
        "positions": positions,
        "layer_norm": gain(ks[2], (DEPTH_2, D_MODEL)),
        "mla_w_in": nrm(ks[3], (N_MLA, D_MODEL, MLA_IN), D_MODEL),
        "mla_q_norm": gain(ks[4], (N_MLA, MLA_Q_RANK)),
        "mla_w_uq": nrm(ks[5], (N_MLA, MLA_Q_RANK, MLA_HEADS * (MLA_NOPE + MLA_ROPE)), MLA_Q_RANK),
        "mla_kv_norm": gain(ks[6], (N_MLA, MLA_KV_RANK)),
        "mla_w_ukv": nrm(ks[7], (N_MLA, MLA_KV_RANK, MLA_HEADS * (MLA_NOPE + MLA_V)), MLA_KV_RANK),
        "mla_w_out": nrm(ks[8], (N_MLA, MLA_WIDTH, D_MODEL), MLA_WIDTH),
        "swa_w_in": nrm(ks[9], (N_SWA, D_MODEL, SWA_IN), D_MODEL),
        "swa_sinks": jax.random.normal(ks[10], (N_SWA, SWA_Q_HEADS), f32),
        "swa_w_out": nrm(ks[11], (N_SWA, SWA_WIDTH, D_MODEL), SWA_WIDTH),
        "final_norm": gain(ks[12], (D_MODEL,)),
    }

def second_block(x, positions, layer_norm, mla_w_in, mla_q_norm, mla_w_uq, mla_kv_norm,
              mla_w_ukv, mla_w_out, swa_w_in, swa_sinks, swa_w_out, final_norm):
    for i in range(DEPTH_2):
        h = rmsnorm(x, layer_norm[i])
        j = i // N_MIXERS
        if i % N_MIXERS == 0:
            y, gate = mla_mixer(h, positions, mla_w_in[j], mla_q_norm[j], mla_w_uq[j],
                                mla_kv_norm[j], mla_w_ukv[j])
            w_out = mla_w_out[j]
        else:
            y, gate = swa_mixer(h, positions, swa_w_in[j], swa_sinks[j])
            w_out = swa_w_out[j]
        x = x + (y * jax.nn.silu(gate)) @ w_out
    return rmsnorm(x, final_norm)


def setup_inputs(seed=0):
    out = dict(first_inputs(seed))
    for name, value in second_inputs(seed + 1).items():
        if name != "x":
            out[name + "_2"] = value
    return out


def reference(
    x, meta_tokens, mix_norm_g, w_in, conv_w, a_log, dt_bias, gdn_norm_g, w_o_gdn, fox_q_norm_g,
    fox_k_norm_g, fox_f_bias, w_o_fox, w_out, mlp_norm_g, w_up, w_down, final_norm_g,
    positions_2, layer_norm_2, mla_w_in_2, mla_q_norm_2, mla_w_uq_2, mla_kv_norm_2, mla_w_ukv_2,
    mla_w_out_2, swa_w_in_2, swa_sinks_2, swa_w_out_2, final_norm_2,
):
    x = first_block(
        x, meta_tokens, mix_norm_g, w_in, conv_w, a_log, dt_bias, gdn_norm_g, w_o_gdn,
        fox_q_norm_g, fox_k_norm_g, fox_f_bias, w_o_fox, w_out, mlp_norm_g, w_up, w_down,
        final_norm_g,
    )
    return second_block(
        x, positions_2, layer_norm_2, mla_w_in_2, mla_q_norm_2, mla_w_uq_2, mla_kv_norm_2,
        mla_w_ukv_2, mla_w_out_2, swa_w_in_2, swa_sinks_2, swa_w_out_2, final_norm_2,
    )


_drawn_inputs = setup_inputs


def setup_inputs(seed=0):
    import zlib

    import numpy as np

    out = dict(_drawn_inputs(seed))
    spreads = {}
    factors = {'mix_norm_g': 4.494,
     'gdn_norm_g': 7.938,
     'fox_q_norm_g': 8.0,
     'fox_k_norm_g': 8.0,
     'mlp_norm_g': 3.083,
     'mla_q_norm_2': 8.0,
     'mla_kv_norm_2': 4.531,
     'swa_sinks_2': 4.992}
    for name, (base, spread) in spreads.items():
        noise = np.random.default_rng([zlib.crc32(name.encode()), seed]).standard_normal(out[name].shape)
        drawn = base * np.exp(spread * noise) if base else spread * noise
        out[name] = __import__('jax').numpy.asarray(drawn.astype(out[name].dtype))
    for name, factor in factors.items():
        out[name] = (out[name] * factor).astype(out[name].dtype)
    return out
```

```python
from contextlib import ExitStack

import numpy as np

import concourse.bass as bass
from concourse import mybir

P = 128
D = 2048
KT = D // P
META, SEQ = 16, 256
TOK = META + SEQ
HEADS = 16
FF = 4 * D
EPS = 1e-6
HALF_KT = 8
SLAB = HALF_KT * P
RING = 4
MLA_RANK = 512
RT = MLA_RANK // P
ROPE_THETA = 500000.0
NEG = -1e30
HEAD_SCALE = float(P) ** -0.5
MLA_SCALE = float(P + 64) ** -0.5
SWA_SCALE = 64.0 ** -0.5
WINDOW = 128
ROUND = 1.5 * 2.0 ** 23
TURN_HI = 6.28125
TURN_LO = float(2 * np.pi - 6.28125)
PI_BELOW = 3.1415925
LEVELS = (1, 2, 4, 8, 16, 32, 64)

F32 = mybir.dt.float32
F32R = mybir.dt.float32r
I32 = mybir.dt.int32
ALU = mybir.AluOpType
ACT = mybir.ActivationFunctionType
AX = mybir.AxisListType

CHUNKS = ((0, META), (META, P), (META + P, P))
MAIN = CHUNKS[1:]
MAIN_FIRST = MAIN + CHUNKS[:1]

SCALARS_SLABS = 2
MIX_TILES = 7
MERGE_TILES = 4
QUARTERS = 4
MLA_IN_TILES = 9
MLA_PAIR_TILES = 8
SWA_KV_TILES = 6


def phase_table():
    phases = [("scalars", 2, 1), ("mix", HEADS * 2 * MIX_TILES, HEADS * MIX_TILES),
              ("merge", KT * 2 * MERGE_TILES, KT * MERGE_TILES), ("out", KT * 2, KT)]
    for q in range(QUARTERS):
        phases += [(f"up{q}", KT * 2, KT), (f"down{q}", KT * 2, KT)]
    phases += [("mla_in", 2 * MLA_IN_TILES, MLA_IN_TILES), ("mla", 8 * 8, 8 * MLA_PAIR_TILES),
               ("mla_out", KT * 2, KT), ("swa_kv", 2 * SWA_KV_TILES, SWA_KV_TILES),
               ("swa", KT * 4, KT * 2), ("swa_out", KT * 2, KT)]
    table, slab, tile = {}, 0, 0
    for name, slabs, tiles in phases:
        table[name] = (slab, tile)
        slab, tile = slab + slabs, tile + tiles
    table["end"] = (slab, tile)
    return table, slab


TABLE, SLABS = phase_table()
STREAM = -(-(SLABS + 2) // RING) * RING


def constants():
    at, parts, n = {}, [], 0

    def add(name, a):
        nonlocal n
        full = np.zeros((P, a.shape[1]), np.float32)
        full[:a.shape[0]] = a
        at[name] = (n, n + a.shape[1])
        parts.append(full)
        n += a.shape[1]

    def blocks(square, below=0.0):
        meta = np.full((P, META), below, np.float32)
        meta[:META] = square[:META, :META]
        return np.concatenate([meta, square, square], axis=1)

    j, i = np.arange(P)[:, None], np.arange(P)[None, :]
    add("identity", blocks(np.eye(P, dtype=np.float32)))
    add("ones", np.ones((P, P), np.float32))
    add("future", blocks(np.where(j > i, np.float32(NEG), np.float32(0)), NEG))
    for b in LEVELS:
        step = (j // (2 * b) == i // (2 * b)) & ((i // b) % 2 == 1) & ((j // b) % 2 == 0)
        add(f"level{b}", blocks(step.astype(np.float32)))
    qi, key = np.arange(P)[:, None], np.arange(TOK)[None, :]
    add("fox0", np.where(key[:, :META + P] <= qi + META, np.float32(0), np.float32(NEG)))
    add("fox1", np.where(key <= qi + META + P, np.float32(0), np.float32(NEG)))
    key = np.arange(SEQ)[None, :]
    first = np.where(key[:, :P] <= qi, np.float32(0), np.float32(NEG))
    add("causal", np.concatenate([first, np.where(key <= qi + P, np.float32(0), np.float32(NEG))], axis=1))
    near = (key <= qi + P) & (qi + P - key < WINDOW)
    add("window", np.concatenate([first, np.where(near, np.float32(0), np.float32(NEG))], axis=1))

    def turn(dim, rot):
        m = np.zeros((P, P), np.float32)
        for r in range(P):
            o, h = r % dim, rot // 2
            if o < h:
                m[r + h, r] = -1
            elif o < rot:
                m[r - h, r] = 1
        return m

    add("turn_mla", turn(64, 64))
    add("turn_swa", turn(64, 16))

    def freq(rot):
        o = np.arange(P) % 64
        inv = np.float32(ROPE_THETA) ** (-(np.arange(0, rot, 2, dtype=np.float32)) / np.float32(rot))
        return np.where(o < rot, inv.astype(np.float32)[o % (rot // 2)], 0).astype(np.float32)[:, None]

    add("freq_mla", freq(64))
    add("freq_swa", freq(16))
    sign = np.ones((P, 1), np.float32)
    sign[64:80] = -1
    add("sign", sign)
    add("eps", np.full((P, 1), EPS, np.float32))
    reset = np.ones((P, TOK), np.float32)
    for start, _ in CHUNKS:
        reset[32:48, start] = 0
    add("reset", reset)
    return np.concatenate(parts, axis=1), at


CONST, CONST_AT = constants()

VEC_AT, VEC_N = {}, 0
for _name, _n in (("mix_norm", KT), ("mlp_norm", KT), ("final_norm", KT), ("layer0", KT), ("layer1", KT),
                  ("final2", KT), ("conv", 48 * 4), ("gdn_norm", 1), ("fox_q", 1), ("fox_k", 1),
                  ("bias", 1), ("a_log", 1), ("mla_q", RT), ("mla_kv", RT), ("sinks", 32)):
    VEC_AT[_name] = (VEC_N, VEC_N + _n)
    VEC_N += _n


def program(nc, stream, consts_in, vecs_in, xT_in, positions_in, rows, out):
    with ExitStack() as ctx:
        cursor = [-(-nc.sbuf_base // 64) * 64]

        def place(name, shape, dt=F32, at=None):
            size = int(np.prod(shape[1:])) * 4
            where = cursor[0] if at is None else at
            if at is None:
                cursor[0] += -(-size // 64) * 64
            return nc.alloc_sbuf_tensor_at(name, list(shape), dt, offset=where)

        def region(size):
            start = cursor[0]
            cursor[0] += size
            return start

        raw = place("raw", [P, RING, SLAB])
        w_hi = place("w_hi", [P, RING, SLAB], F32R)
        w_lo = place("w_lo", [P, RING, SLAB], F32R)
        u_hi = place("u_hi", [P, KT, TOK], F32R)
        u_lo = place("u_lo", [P, KT, TOK], F32R)
        ya_at = region(2 * KT * SEQ * 4)
        ya_hi = place("ya_hi", [P, KT, SEQ], F32R, ya_at)
        ya_lo = place("ya_lo", [P, KT, SEQ], F32R, ya_at + KT * SEQ * 4)
        yb_at = region(2 * KT * SEQ * 4)
        yb_hi = place("yb_hi", [P, KT, SEQ], F32R, yb_at)
        yb_lo = place("yb_lo", [P, KT, SEQ], F32R, yb_at + KT * SEQ * 4)
        h = place("h", [P, KT, SEQ], F32, yb_at)
        mx_at = region(2 * KT * SEQ * 4)
        mx_hi = place("mx_hi", [P, KT, SEQ], F32R, mx_at)
        mx_lo = place("mx_lo", [P, KT, SEQ], F32R, mx_at + KT * SEQ * 4)
        xT = place("xT", [P, KT, TOK], F32, mx_at)
        consts = place("consts", [P, CONST.shape[1]])
        vecs = place("vecs", [P, VEC_N])
        tokcol = place("tokcol", [P, 3, 4, 32])
        top = cursor[0]

        def const(name, lo=0, hi=None, rows_=P):
            a, b = CONST_AT[name]
            return consts[0:rows_, a + lo:(b if hi is None else a + hi)]

        def vec(name, k=0, n=1):
            a = VEC_AT[name][0] + k
            return vecs[:, a:a + n]

        class Temps:

            def __init__(self, tag, spans):
                self.tag, self.spans = tag, [list(s) for s in spans]

            def __call__(self, name, shape, dt=F32):
                size = -(-int(np.prod(shape[1:])) * 4 // 64) * 64
                for s in self.spans:
                    if s[0] + size <= s[1]:
                        s[0] += size
                        return nc.alloc_sbuf_tensor_at(f"{self.tag}_{name}", list(shape), dt, offset=s[0] - size)
                raise AssertionError((self.tag, name))

        mx_span = (mx_at, mx_at + 2 * KT * SEQ * 4)
        end_span = (top, nc.sbuf_usable_end // 64 * 64)

        bank = [ctx.enter_context(nc.psum_tensor(f"bank{b}", [P, 512], F32)) for b in range(8)]
        proj = bank[0:2]

        named = {}

        def sem(name):
            if name not in named:
                named[name] = ctx.enter_context(nc.semaphore(name.replace(" ", "_")))
            return named[name]

        landed = [sem(f"slab {r} landed") for r in range(RING)]
        hi_ready, lo_ready, slab_used = sem("w_hi ready"), sem("w_lo ready"), sem("slab used")
        inputs_in = sem("inputs in")
        tile_free = [sem(f"proj {b} free") for b in range(2)]

        def slab_no(phase, n, i=None, per=0):
            m = TABLE[phase][0] + n
            assert per % RING == 0
            if i is None:
                return m, m % RING, m // RING
            return m + i * per, m % RING, m // RING + i * (per // RING)

        def split_hi(act, phase, n, i=None, per=0):
            m, slot, turn = slab_no(phase, n, i, per)
            act.wait_ge(landed[slot], (turn + 1) * 16)
            act.wait_ge(slab_used, m + 1)
            act.activation(w_hi[:, slot], raw[:, slot], ACT.Copy).then_inc(hi_ready, 1)

        def split_lo(dve, phase, n, i=None, per=0):
            m, slot, _ = slab_no(phase, n, i, per)
            dve.wait_ge(hi_ready, m + 1)
            dve.tensor_tensor(w_lo[:, slot], raw[:, slot], w_hi[:, slot].bitcast(F32),
                              ALU.subtract).then_inc(lo_ready, 1)

        def tile_no(phase, n, i=None, per=0):
            t = TABLE[phase][1] + n
            assert per % 2 == 0
            if i is None:
                return t % 2, t // 2
            return t % 2, t // 2 + i * (per // 2)

        def await_slab(eng, phase, n, i=None, per=0):
            eng.wait_ge(slab_used, slab_no(phase, n, i, per)[0] + 1 + RING)

        def await_tiles_out(eng, phase):
            t = TABLE[phase][1]
            for b in range(2):
                eng.wait_ge(tile_free[b], (t + 1 - b) // 2 + 1)

        def products(pe, phase, slab, o, x, first, last, i=None, per=0):
            m, slot, _ = slab_no(phase, slab, i, per)
            pe.wait_ge(lo_ready, m + 1)
            for k in range(HALF_KT):
                a, b = w_hi[:, slot, k * P:(k + 1) * P], w_lo[:, slot, k * P:(k + 1) * P]
                x_hi, x_lo = x(k if first else HALF_KT + k)
                pe.matmul(o, a, x_hi, start=first and k == 0, stop=False)
                pe.matmul(o, a, x_lo, start=False, stop=False)
                mm = pe.matmul(o, b, x_hi, start=False, stop=last and k == HALF_KT - 1)
            mm.then_inc(slab_used, 1)

        def full_tile(pe, phase, n, x, width, slab, i=None, slabs_per=0, tiles_per=0):
            b, turn = tile_no(phase, n, i, tiles_per)
            pe.wait_ge(tile_free[b], turn + 1)
            o = proj[b][:, 0:width]
            products(pe, phase, slab, o, x, True, False, i, slabs_per)
            products(pe, phase, slab + 1, o, x, False, True, i, slabs_per)

        def u_all(k):
            return u_hi[:, k, :], u_lo[:, k, :]

        def u_seq(k):
            return u_hi[:, k, META:], u_lo[:, k, META:]

        def ya(k):
            return ya_hi[:, k], ya_lo[:, k]

        def yb(k):
            return yb_hi[:, k], yb_lo[:, k]

        def mx(k):
            return mx_hi[:, k], mx_lo[:, k]

        norm_t = Temps("norm", [(ya_at, ya_at + 2 * KT * SEQ * 4)])
        norm_sq, norm_v = norm_t("sq", [P, 4, TOK]), norm_t("v", [P, 4, TOK])
        norm_ln, norm_rs = norm_t("ln", [P, TOK]), norm_t("rs", [P, TOK])

        def norm_act(act, nu, src, width, split):
            w = width
            if nu:
                act.wait_ge(sem("norm done"), nu)
            for k in range(KT):
                if k >= 4:
                    act.wait_ge(sem("norm sq used"), nu * KT + k - 3)
                act.activation(norm_sq[:, k % 4, :w], src[:, k, :w], ACT.Square).then_inc(sem("norm sq"), 1)
            act.wait_ge(sem("norm sq used"), (nu + 1) * KT)
            act.activation(norm_ln[:, :w], bank[2][:, :w], ACT.Ln, scale=1.0 / D,
                           bias=const("eps")).then_inc(sem("norm ln"), 1)
            act.wait_ge(sem("norm ln"), nu + 1)
            act.activation(norm_rs[:, :w], norm_ln[:, :w], ACT.Exp, scale=-0.5).then_inc(sem("norm rs"), 1)
            if split is not None:
                for k in range(KT):
                    act.wait_ge(sem("norm v"), split * KT + k + 1)
                    act.activation(u_hi[:, k, TOK - w:], norm_v[:, k % 4, :w],
                                   ACT.Copy).then_inc(sem("norm hi"), 1)

        def norm_pe(pe, nu, width):
            for k in range(KT):
                pe.wait_ge(sem("norm sq"), nu * KT + k + 1)
                pe.matmul(bank[2][:, :width], const("ones"), norm_sq[:, k % 4, :width], start=k == 0,
                          stop=k == KT - 1).then_inc(sem("norm sq used"), 1)

        def norm_dve(dve, nu, src, width, gain, split):
            w = width
            dve.wait_ge(sem("norm rs"), nu + 1)
            if split is None:
                for k in range(KT):
                    ins = dve.scalar_tensor_tensor(out=src[:, k, :w], in0=src[:, k, :w], scalar=vec(gain, k),
                                                   in1=norm_rs[:, :w], op0=ALU.mult, op1=ALU.mult)
                    ins.then_inc(sem("norm in place"), 1)
                dve.wait_ge(sem("norm in place"), KT * (1 if nu < 5 else 2))
                dve.sem_inc(sem("norm done"), 1)
                return
            for k in range(KT + 1):
                if k < KT:
                    if k >= 4:
                        dve.wait_ge(sem("norm lo"), split * KT + k - 3)
                    dve.scalar_tensor_tensor(out=norm_v[:, k % 4, :w], in0=src[:, k, :w], scalar=vec(gain, k),
                                             in1=norm_rs[:, :w], op0=ALU.mult,
                                             op1=ALU.mult).then_inc(sem("norm v"), 1)
                if k:
                    dve.wait_ge(sem("norm hi"), split * KT + k)
                    dve.tensor_tensor(u_lo[:, k - 1, TOK - w:], norm_v[:, (k - 1) % 4, :w],
                                      u_hi[:, k - 1, TOK - w:].bitcast(F32), ALU.subtract).then_inc(sem("norm lo"), 1)
            dve.wait_ge(sem("norm lo"), (split + 1) * KT)
            dve.sem_inc(sem("norm done"), 1)

        mt = Temps("mix", [mx_span, end_span])
        conv_in = [mt(f"conv_in_{x}", [P, 3 + TOK]) for x in "kvq"]
        kT, vT, qT = (mt(x, [P, TOK]) for x in ("kT", "vT", "qT"))
        gate_th = mt("th", [P, TOK])
        z_raw = mt("z_raw", [P, SEQ])
        fq, fk, fv = mt("fq", [P, SEQ]), mt("fk", [P, TOK]), mt("fv", [P, TOK])
        sq, ln_t, rs_t = mt("sq", [P, TOK]), mt("ln", [P, TOK]), mt("rs", [P, TOK])
        q_dec = mt("q_dec", [P, SEQ])
        row = mt("row", [P, 3, TOK])
        g_exp, decay = mt("g_exp", [P, TOK]), mt("decay", [P, TOK])
        b_mat, qk, b_step = mt("b_mat", [P, TOK]), mt("qk", [P, TOK]), mt("b_step", [P, TOK])
        inv, inv_t, prod = mt("inv", [P, TOK]), mt("inv_t", [P, TOK]), mt("prod", [P, TOK])
        k_dec, k_dec_m = mt("k_dec", [P, 2, P]), mt("k_dec_m", [META, P])
        v_beta, v_beta_m = mt("v_beta", [P, 2, P]), mt("v_beta_m", [META, P])
        state, rhs, v_new = mt("state", [P, P]), mt("rhs", [P, P]), mt("v_new", [P, P])
        v_new_m = mt("v_new_m", [META, P])
        y_out = mt("y_out", [P, SEQ])
        f_bias, f_p = mt("f_bias", [P, META + P + TOK]), mt("f_p", [P, META + P + TOK])
        f_pt, f_pt_m = mt("f_pt", [P, 3 * P]), mt("f_pt_m", [META, SEQ])
        f_v, f_v_m = mt("f_v", [P, 2, P]), mt("f_v_m", [META, P])
        col = mt("col", [P, 3, 4])
        half_beta, neg_beta_eg, to_last, neg_g, eg_col = (mt(x, [P, 3]) for x in
                                                          ("half_beta", "neg_beta_eg", "to_last", "neg_g", "eg_col"))
        eg_last = mt("eg_last", [P, 2])
        f_max, f_sum, f_inv = mt("f_max", [P, 2]), mt("f_sum", [P, 2]), mt("f_inv", [P, 2])
        FW = (META + P, TOK)
        F_AT = (0, META + P)

        MB = 2 * MIX_TILES

        def norm_of_head(name, n):
            return n * 5 - 4 + ("gdn k", "gdn q", "gdn o", "fox q", "fox k").index(name)

        ORDER = {"k": 0, "v": 1, "q": 2, "z": 3, "fq": 4, "fk": 5, "fv": 6}

        sc = Temps("scalars", [(ya_at + 16384, ya_at + 2 * KT * SEQ * 4)])
        sc_x, sc_xs, sc_out, sc_rate = (sc("x", [P, TOK]), sc("xs", [P, TOK]), sc("out", [P, TOK]),
                                        sc("rate", [P, 1]))
        sc_t = [sc(f"t{k}", [P, TOK]) for k in range(4)]

        gt = Temps("merge", [end_span])
        sig_a, sig_b, mix_a, mix_b, mix_v = (gt(x, [P, SEQ]) for x in ("sig_a", "sig_b", "mix_a", "mix_b", "mix_v"))
        ft = Temps("mlp", [mx_span])
        relu_t, hid_v = ft("relu", [P, 2, SEQ]), ft("hid", [P, 2, SEQ])
        at = Temps("att", [mx_span, (yb_at + KT * SEQ * 4, yb_at + 2 * KT * SEQ * 4), end_span])
        c_at = mx_at
        c_hi, c_lo = at("c_hi", [P, 2 * RT, SEQ], F32R), at("c_lo", [P, 2 * RT, SEQ], F32R)
        c_raw = at("c_raw", [P, 2 * RT, SEQ])
        pos_i = at("pos_i", [P, SEQ], I32)
        pos_f, angle, turns, reduced = (at(x, [P, SEQ]) for x in ("pos_f", "angle", "turns", "reduced"))
        cos_sin = {x: (at("cos_" + x, [P, SEQ]), at("sin_" + x, [P, SEQ])) for x in ("mla", "swa")}
        k_rope = at("k_rope", [P, SEQ])
        gate_s = at("gate_s", [P, 2, SEQ])
        gate_t = at("gate_t", [P, SEQ])
        q_m, k_m, v_m = (at(x, [P, 2, SEQ]) for x in ("q_m", "k_m", "v_m"))
        q_rope, rope_a, rope_b = (at(x, [P, SEQ]) for x in ("q_rope", "rope_a", "rope_b"))
        logits, probs, probs_t = (at(x, [P, 3 * P]) for x in ("logits", "probs", "probs_t"))
        row_max, row_sum, row_inv, row_sink = (at(x, [P, 2]) for x in ("row_max", "row_sum", "row_inv", "row_sink"))
        v_tok = at("v_tok", [P, 2, P])
        y_v = at("y_v", [P, SEQ])
        wt = Temps("swa", [(c_at, c_at + 6 * RT * SEQ * 4)])
        k_s = wt("k_s", [P, 4, SEQ])
        v_raw = wt("v_raw", [P, 2, SEQ])
        v_all = wt("v_all", [P, 2, 4, 64])
        k_own, v_own = wt("k_own", [P, SEQ]), wt("v_own", [P, 2, 64])
        sink, neg_sink = wt("sink", [P, 8]), wt("neg_sink", [P, 8])
        s_gate, s_th, s_y = (wt(x, [P, SEQ]) for x in ("gate", "th", "y"))
        q_s = wt("q_s", [P, SEQ])
        heads_before = {"mla": 0, "swa": HEADS}
        SWA_K_TURNS = 1 + HEADS // 2 + 1
        SWA_Q_TURNS = SWA_K_TURNS + 3
        W_AT, W_W = (0, P), (P, SEQ)

        block = ctx.enter_context(nc.Block())

        @block.sync
        def _(sp):
            for r in range(RING):
                sp.dma_start(raw[:, r], stream[r]).then_inc(landed[r], 16)
            with sp.Fori(1, STREAM // RING) as i:
                for r in range(RING):
                    sp.wait_ge(lo_ready, i * RING - RING + r + 1)
                    sp.dma_start(raw[:, r], stream[i * RING + r]).then_inc(landed[r], 16)
            sp.wait_ge(sem("norm done"), 6)
            sp.dma_start(out, h[:]).then_inc(sem("out written"), 16)
            sp.wait_ge(sem("out written"), 16)
            loads = STREAM // RING
            for r in range(RING):
                sp.wait_ge(landed[r], 16 * loads)

        @block.gpsimd
        def _(gp):
            gp.dma_start(consts[:], consts_in).then_inc(inputs_in, 16)
            gp.dma_start(vecs[:], vecs_in).then_inc(inputs_in, 16)
            gp.dma_start(xT[:], xT_in).then_inc(sem("x in"), 16)
            gp.wait_ge(sem("scalars"), 2)
            gp.dma_start(rows, sc_out[:]).then_inc(sem("rows out"), 16)
            gp.wait_ge(sem("rows out"), 16)
            by_head = rows.rearrange("(g r) n -> r g n", g=4)
            with gp.Fori(0, HEADS) as hd:
                gp.wait_ge(sem("row free"), hd + 1)
                gp.dma_start(row[:], by_head[bass.ts(hd, 1), 0:3, :].rearrange("a g n -> (a g) n")
                             .partition_broadcast(P)).then_inc(sem("row in"), 16)
            await_slab(gp, "out", -1)
            gp.dma_start(h[:], xT_in[:, :, META:]).then_inc(sem("h in"), 16)
            await_slab(gp, "mla_in", -1)
            gp.dma_start(pos_i[:], positions_in.partition_broadcast(P).rearrange("p a n -> p (a n)")).then_inc(
                sem("positions in"), 16)

        @block.tensor
        def _(pe):
            ident = const("identity", META, META + P)
            pe.sem_inc(slab_used, RING)
            for b in range(2):
                pe.sem_inc(tile_free[b], 1)
            pe.wait_ge(inputs_in, 32)
            norm_pe(pe, 0, TOK)
            pe.wait_ge(sem("norm lo"), KT)
            full_tile(pe, "scalars", 0, u_all, TOK, 0)
            pe.wait_ge(sem("scalars"), 2)
            for c, (t0, w) in enumerate(CHUNKS):
                mm = pe.transpose(bank[3][0:w, c * P:(c + 1) * P], sc_out[:, t0:t0 + w], ident)
            mm.then_inc(sem("scalar columns"), 1)

            def ones_sum(name, n, src, width, b=2):
                pe.wait_ge(sem("length sq"), norm_of_head(name, n))
                pe.matmul(bank[b][:, :width], const("ones"), src[:, :width], start=True,
                          stop=True).then_inc(sem("length sum"), 1)

            def gdn(n):
                ones_sum("gdn k", n, sq, TOK)
                ones_sum("gdn q", n, sq, TOK)
                pe.wait_ge(sem("k unit"), n)
                for c, (t0, w) in enumerate(CHUNKS):
                    o = bank[3][0:w, (c - 1) * P:c * P] if c else bank[3][0:w, 2 * P:3 * P]
                    mm = pe.transpose(o, kT[:, t0:t0 + w], ident)
                mm.then_inc(sem("k turned"), 1)
                pe.wait_ge(sem("silu"), n * 4 - 2)
                for c, (t0, w) in enumerate(CHUNKS):
                    o = bank[4][0:w, (c - 1) * P:c * P] if c else bank[4][0:w, 2 * P:3 * P]
                    mm = pe.transpose(o, vT[:, t0:t0 + w], ident)
                mm.then_inc(sem("v turned"), 1)
                for t0, w in MAIN_FIRST:
                    mm = pe.matmul(bank[5][0:w, t0:t0 + w], kT[:, t0:t0 + w], kT[:, t0:t0 + w], start=True,
                                   stop=True)
                mm.then_inc(sem("kk"), 1)
                pe.wait_ge(sem("q unit"), n)
                for c, (t0, w) in enumerate(MAIN):
                    mm = pe.matmul(bank[6][0:w, t0:t0 + w], kT[:, t0:t0 + w], qT[:, t0:t0 + w], start=True,
                                   stop=True)
                mm.then_inc(sem("qk"), 1)
                for lv, b in enumerate(LEVELS):
                    spans = MAIN_FIRST if b < META else MAIN
                    at = (n - 1) * len(LEVELS) + lv + 1
                    pe.wait_ge(sem("b step"), at)
                    if lv:
                        pe.wait_ge(sem("inverse"), (n - 1) * 13 + 2 * lv)
                    for t0, w in spans:
                        right = inv[0:w, t0:t0 + w] if lv else const("identity", t0, t0 + w, w)
                        mm = pe.matmul(bank[5][0:w, t0:t0 + w], b_step[0:w, t0:t0 + w], right, start=True,
                                       stop=True)
                    mm.then_inc(sem("prod sum"), 1)
                    if not lv:
                        continue
                    pe.wait_ge(sem("prod"), (n - 1) * 6 + lv)
                    if b != LEVELS[-1]:
                        for t0, w in spans:
                            mm = pe.matmul(bank[6][0:w, t0:t0 + w], inv_t[0:w, t0:t0 + w],
                                           prod[0:w, t0:t0 + w], start=True, stop=True)
                        mm.then_inc(sem("step"), 1)
                    for t0, w in spans:
                        mm = pe.matmul(bank[7][0:w, t0:t0 + w], prod[0:w, t0:t0 + w],
                                       inv_t[0:w, t0:t0 + w], start=True, stop=True)
                    mm.then_inc(sem("step t"), 1)
                pe.wait_ge(sem("inverse"), (n - 1) * 13 + 13)
                pe.wait_ge(sem("v beta"), 3 * n)
                pe.matmul(bank[3][:, 0:P], inv_t[0:META, 0:P], v_beta_m[:, :], start=True,
                          stop=True).then_inc(sem("v new m sum"), 1)
                pe.wait_ge(sem("k dec"), 3 * n)
                pe.wait_ge(sem("v new m"), n)
                pe.matmul(bank[3][:, P:2 * P], k_dec_m[:, :], v_new_m[:, :], start=True,
                          stop=True).then_inc(sem("state sum"), 1)
                for c, (t0, w) in enumerate(MAIN):
                    pe.wait_ge(sem("state"), 2 * n - 1 + c)
                    pe.matmul(bank[4][:, 0:P], kT[:, t0:t0 + w], state[:, :], start=True,
                              stop=True).then_inc(sem("k state"), 1)
                    pe.wait_ge(sem("rhs"), 2 * n - 1 + c)
                    pe.matmul(bank[4][:, P:2 * P], inv_t[:, t0:t0 + w], rhs[:, :], start=True,
                              stop=True).then_inc(sem("v new sum"), 1)
                    o = bank[6][:, c * P:(c + 1) * P]
                    pe.wait_ge(sem("q dec"), n)
                    pe.matmul(o, state[:, :], q_dec[:, c * P:(c + 1) * P], start=True, stop=False)
                    pe.wait_ge(sem("v new"), 2 * n - 1 + c)
                    pe.matmul(o, v_new[:, :], qk[:, t0:t0 + w], start=False, stop=True).then_inc(
                        sem("gdn o"), 1)
                    if c == 0:
                        pe.matmul(bank[3][:, P:2 * P], k_dec[:, 0], v_new[:, :], start=True,
                                  stop=True).then_inc(sem("state sum"), 1)
                ones_sum("gdn o", n, sq, SEQ)

            def fox(n):
                ones_sum("fox q", n, sq, SEQ)
                ones_sum("fox k", n, sq, TOK)
                for c, (t0, w) in enumerate(CHUNKS):
                    o = bank[3][0:w, (c - 1) * P:c * P] if c else bank[3][0:w, 2 * P:3 * P]
                    mm = pe.transpose(o, fv[:, t0:t0 + w], ident)
                mm.then_inc(sem("fox v turned"), 1)
                pe.wait_ge(sem("fox qk unit"), 2 * n)
                for t in range(2):
                    mm = pe.matmul(bank[4][:, F_AT[t]:F_AT[t] + FW[t]], fq[:, t * P:(t + 1) * P],
                                   fk[:, 0:FW[t]], start=True, stop=True)
                mm.then_inc(sem("fox s"), 1)
                pe.wait_ge(sem("fox p"), 2 * n)
                pe.transpose(bank[5][:, 0:P], f_p[:, META:META + P], ident)
                pe.transpose(bank[5][:, P:2 * P], f_p[:, F_AT[1] + META:F_AT[1] + META + P], ident)
                pe.transpose(bank[5][:, 2 * P:3 * P], f_p[:, F_AT[1] + META + P:F_AT[1] + TOK], ident)
                pe.transpose(bank[6][0:META, 0:P], f_p[:, 0:META], ident)
                pe.transpose(bank[6][0:META, P:2 * P], f_p[:, F_AT[1]:F_AT[1] + META],
                             ident).then_inc(sem("fox p turned"), 1)
                pe.wait_ge(sem("fox pt"), 2 * n)
                pe.wait_ge(sem("fox v"), 2 * n)
                pe.matmul(bank[7][:, 0:SEQ], f_v_m[:, :], f_pt_m[:, :], start=True, stop=False)
                pe.matmul(bank[7][:, P:SEQ], f_v[:, 1], f_pt[:, SEQ:3 * P], start=False, stop=False,
                          skip_group_check=True)
                pe.matmul(bank[7][:, 0:SEQ], f_v[:, 0], f_pt[:, 0:SEQ], start=False,
                          stop=True).then_inc(sem("fox o"), 1)

            with pe.Fori(0, HEADS // 2) as i:
                for s in range(2):
                    n = i * 2 + s + 1
                    for j in range(MIX_TILES):
                        seq = j in (ORDER["z"], ORDER["fq"])
                        full_tile(pe, "mix", s * MIX_TILES + j, u_seq if seq else u_all, SEQ if seq else TOK,
                                  s * MB + 2 * j, i, 2 * MB, 2 * MIX_TILES)
                    gdn(n)
                    fox(n)
            pe.wait_ge(sem("ya lo"), HEADS)
            pe.wait_ge(sem("yb lo"), HEADS)
            with pe.Fori(0, KT) as i:
                for j, x in enumerate((u_seq, u_seq, ya, yb)):
                    full_tile(pe, "merge", j, x, SEQ, 2 * j, i, 8, 4)

            def matrix(phase, x):
                with pe.Fori(0, KT // 2) as i:
                    for s in range(2):
                        full_tile(pe, phase, s, x, SEQ, 2 * s, i, 4, 2)

            pe.wait_ge(sem("mix lo"), KT)
            matrix("out", mx)
            norm_pe(pe, 1, SEQ)
            pe.wait_ge(sem("norm lo"), 2 * KT)
            for q in range(QUARTERS):
                matrix(f"up{q}", u_seq)
                pe.wait_ge(sem("hidden lo"), (q + 1) * KT)
                matrix(f"down{q}", ya)
            norm_pe(pe, 2, SEQ)
            norm_pe(pe, 3, SEQ)
            pe.wait_ge(sem("norm lo"), 3 * KT)
            for t in range(MLA_IN_TILES):
                full_tile(pe, "mla_in", t, u_seq, SEQ, 2 * t)
            for g in range(2):
                for k in range(RT):
                    pe.wait_ge(sem("c sq"), g * RT + k + 1)
                    pe.matmul(bank[2][:, :SEQ], const("ones"), norm_sq[:, k, :SEQ], start=k == 0,
                              stop=k == RT - 1).then_inc(sem("c sum"), 1)
            pe.matmul(bank[6][:, :SEQ], const("turn_mla"), k_rope[:], start=True, stop=True).then_inc(
                sem("turned half"), 1)

            def softmax_pe(tag, c, scores, value, o):
                c = heads_before[tag] + c
                scores()
                pe.wait_ge(sem("head p"), 2 * c)
                pe.transpose(bank[3][:, 0:P], probs[:, 0:P], ident)
                pe.transpose(bank[3][:, P:2 * P], probs[:, P:2 * P], ident)
                pe.transpose(bank[3][:, 2 * P:3 * P], probs[:, 2 * P:3 * P], ident).then_inc(
                    sem("head p turned"), 1)
                pe.wait_ge(sem("head pt"), c)
                pe.matmul(o[:, 0:P], value(0), probs_t[:, 0:P], start=True, stop=True)
                pe.matmul(o[:, P:SEQ], value(0), probs_t[:, P:2 * P], start=True, stop=False)
                pe.matmul(o[:, P:SEQ], value(1), probs_t[:, 2 * P:3 * P], start=False, stop=True).then_inc(
                    sem("head o"), 1)

            pe.wait_ge(sem("c lo"), 2 * RT)
            pe.wait_ge(sem("rotated"), 1)
            with pe.Fori(0, HEADS // 2) as i:
                for s in range(2):
                    full_tile(pe, "mla", s, u_seq, SEQ, 2 * s, i, 8, 8)

                def small_tile(slab, s, o, x0):
                    _, slot, _ = slab_no("mla", slab, i, 8)
                    for k in range(RT):
                        e = (s * RT + k) * P
                        pe.matmul(o, w_hi[:, slot, e:e + P], c_hi[:, x0 + k], start=k == 0, stop=False)
                        pe.matmul(o, w_hi[:, slot, e:e + P], c_lo[:, x0 + k], start=False, stop=False)
                        mm = pe.matmul(o, w_lo[:, slot, e:e + P], c_hi[:, x0 + k], start=False,
                                       stop=k == RT - 1)
                    return mm

                for j in range(3):
                    pe.wait_ge(lo_ready, slab_no("mla", 4 + j, i, 8)[0] + 1)
                    for s in range(2):
                        b, turn = tile_no("mla", 2 + 2 * j + s, i, 8)
                        pe.wait_ge(tile_free[b], turn + 1)
                        small_tile(4 + j, s, proj[b][:, 0:SEQ], 0 if j == 0 else RT).then_inc(
                            slab_used if s else sem("mla first half"), 1)
                pe.wait_ge(lo_ready, slab_no("mla", 7, i, 8)[0] + 1)
                pe.wait_ge(sem("mla qr free"), i + 1)
                small_tile(7, 0, bank[7][:, 0:SEQ], 0).then_inc(slab_used, 1)
                pe.wait_ge(sem("mla qr"), i + 1)
                pe.matmul(bank[6][:, :SEQ], const("turn_mla"), q_rope[:], start=True, stop=True).then_inc(
                    sem("turned half"), 1)
                for s in range(2):
                    c = i * 2 + s + 1

                    def scores():
                        if s == 0:
                            pe.wait_ge(sem("rotated"), i + 2)
                        r = slice(64 * s, 64 * s + 64)
                        for t in range(2):
                            o = bank[2][:, W_AT[t]:W_AT[t] + W_W[t]]
                            pe.matmul(o, q_m[:, s, t * P:(t + 1) * P], k_m[:, s, 0:W_W[t]], start=True, stop=False)
                            mm = pe.matmul(o, q_rope[r, t * P:(t + 1) * P], k_rope[r, 0:W_W[t]], start=False,
                                           stop=True)
                        mm.then_inc(sem("head s"), 1)
                        for t in range(2):
                            mm = pe.transpose(bank[4][:, t * P:(t + 1) * P], v_m[:, s, t * P:(t + 1) * P], ident)
                        mm.then_inc(sem("mla v turned"), 1)
                        pe.wait_ge(sem("mla v"), c)

                    softmax_pe("mla", c, scores, lambda t: v_tok[:, t], bank[5])
            pe.wait_ge(sem("mla lo"), HEADS)
            matrix("mla_out", ya)
            norm_pe(pe, 4, SEQ)
            pe.wait_ge(sem("norm lo"), 4 * KT)
            for t in range(SWA_KV_TILES):
                full_tile(pe, "swa_kv", t, u_seq, SEQ, 2 * t)
            for t in range(SWA_KV_TILES):
                b, turn = tile_no("swa_kv", t)
                pe.wait_ge(tile_free[b], turn + 2)
            for t in range(4):
                if t:
                    pe.wait_ge(sem("rotated"), t + SWA_K_TURNS - 1)
                pe.matmul(bank[6][:, :SEQ], const("turn_swa"), k_s[:, t], start=True, stop=True).then_inc(
                    sem("turned half"), 1)
            for t in range(2):
                for m in range(2):
                    mm = pe.transpose(bank[4][:, (2 * t + m) * P:(2 * t + m + 1) * P],
                                      v_raw[:, m, t * P:(t + 1) * P], ident)
            mm.then_inc(sem("swa v turned"), 1)
            with pe.Fori(0, 4) as i:
                for j in range(4):
                    full_tile(pe, "swa", 2 * j, u_seq, SEQ, 4 * j, i, 16, 8)
                    full_tile(pe, "swa", 2 * j + 1, u_seq, SEQ, 4 * j + 2, i, 16, 8)
                    n = i * 4 + j + 1
                    b, turn = tile_no("swa", 2 * j, i, 8)
                    pe.wait_ge(tile_free[b], turn + 2)
                    pe.matmul(bank[6][:, :SEQ], const("turn_swa"), q_s[:], start=True, stop=True).then_inc(
                        sem("turned half"), 1)
                    for s in range(2):
                        c = i * 8 + j * 2 + s + 1

                        def scores():
                            r = slice(64 * s, 64 * s + 64)
                            if s == 0:
                                pe.wait_ge(sem("rotated"), n + SWA_Q_TURNS)
                            for t in range(2):
                                mm = pe.matmul(bank[2][:, W_AT[t]:W_AT[t] + W_W[t]], q_s[r, t * P:(t + 1) * P],
                                               k_own[r, 0:W_W[t]], start=True, stop=True)
                            mm.then_inc(sem("head s"), 1)

                        softmax_pe("swa", c, scores, lambda t: v_own[:, t], bank[5][64 * s:64 * s + 64])
            pe.wait_ge(sem("swa lo"), KT)
            matrix("swa_out", ya)
            norm_pe(pe, 5, SEQ)

        @block.scalar
        def _(act):
            act.wait_ge(inputs_in, 32)
            act.wait_ge(sem("x in"), 16)
            act.preload_act_table_set("natural_log_exp_and_others")
            norm_act(act, 0, xT, TOK, 0)
            split_hi(act, "scalars", 0)
            split_hi(act, "scalars", 1)
            split_hi(act, "scalars", 2)
            split_hi(act, "scalars", 3)
            act.wait_ge(sem("sc dve"), 1)
            act.activation(sc_t[0][:], sc_xs[:], ACT.Abs).then_inc(sem("sc act"), 1)
            act.wait_ge(sem("sc act"), 1)
            act.activation(sc_t[1][:], sc_t[0][:], ACT.Exp, scale=-1.0).then_inc(sem("sc act"), 1)
            act.activation(sc_rate[:], vec("a_log"), ACT.Exp).then_inc(sem("sc act"), 1)
            act.wait_ge(sem("sc act"), 2)
            act.activation(sc_t[2][:], sc_t[1][:], ACT.Ln, bias=1.0).then_inc(sem("sc act"), 1)
            act.activation(sc_t[3][:], sc_x[:], ACT.Tanh, scale=0.5).then_inc(sem("sc act"), 1)
            for c, (t0, w) in enumerate(CHUNKS):
                act.wait_ge(sem("scalar columns"), 1)
                act.activation(tokcol[0:w, c], bank[3][0:w, c * P:(c + 1) * P].rearrange(
                    "p (g r) -> p g r", g=4), ACT.Copy).then_inc(sem("tokcol"), 1)

            def rsqrt(name, n, width, scale, b=2):
                at_ = norm_of_head(name, n)
                act.wait_ge(sem("length sum"), at_)
                act.activation(ln_t[:, :width], bank[b][:, :width], ACT.Ln, scale=scale,
                               bias=const("eps")).then_inc(sem("length ln"), 1)
                act.wait_ge(sem("length ln"), at_)
                act.activation(rs_t[:, :width], ln_t[:, :width], ACT.Exp, scale=-0.5).then_inc(
                    sem("length rs"), 1)

            def gdn_act(n):
                for c, (x, y) in enumerate((("k", kT), ("v", vT), ("q", qT))):
                    act.wait_ge(sem("conv"), n * 12 - 8 + 4 * c)
                    if c:
                        act.wait_ge(sem("silu"), n * 4 - 4 + c)
                    act.activation(gate_th[:], y[:], ACT.Tanh, scale=0.5).then_inc(sem("silu tanh"), 1)
                act.wait_ge(sem("silu"), n * 4 - 1)
                act.activation(gate_th[:, :SEQ], z_raw[:], ACT.Tanh, scale=0.5).then_inc(sem("silu tanh"), 1)
                act.preload_act_table_set("natural_log_exp_and_others")
                act.wait_ge(sem("col"), n)
                act.wait_ge(sem("row in"), n * 16)
                act.activation(half_beta[:], col[:, :, 0], ACT.Copy, scale=0.5).then_inc(sem("cols"), 1)
                act.activation(neg_g[:], col[:, :, 1], ACT.Copy, scale=-1.0).then_inc(sem("cols"), 1)
                act.activation(eg_col[:], col[:, :, 1], ACT.Exp).then_inc(sem("cols"), 1)
                for c, (t0, w) in enumerate(CHUNKS):
                    act.activation(to_last[:, c:c + 1], col[:, c, 1:2], ACT.Exp, scale=-1.0,
                                   bias=row[:, 1, t0 + w - 1:t0 + w]).then_inc(sem("cols"), 1)
                act.activation(eg_last[:, 0:1], row[:, 1, META + P - 1:META + P],
                               ACT.Exp).then_inc(sem("cols"), 1)
                act.activation(g_exp[:], row[:, 1], ACT.Exp).then_inc(sem("g exp"), 1)
                act.wait_ge(sem("cols"), 7 * n)
                act.wait_ge(sem("g diff"), n)
                for c, (t0, w) in enumerate(CHUNKS):
                    act.activation(decay[:, t0:t0 + w], b_step[:, t0:t0 + w], ACT.Exp,
                                   bias=neg_g[:, c:c + 1]).then_inc(sem("decay"), 1)
                for x, y in (("k", kT), ("q", qT)):
                    act.wait_ge(sem("silu"), n * 4 - 3 + (0 if x == "k" else 2))
                    if x == "q":
                        act.wait_ge(sem("length sum"), norm_of_head("gdn k", n))
                        act.wait_ge(sem("k unit"), n)
                    act.activation(sq[:], y[:], ACT.Square, scale=0.5).then_inc(sem("length sq"), 1)
                    rsqrt("gdn " + x, n, TOK, 1.0)
                act.wait_ge(sem("k turned"), n)
                act.activation(k_dec_m[:, :], bank[3][0:META, 2 * P:3 * P], ACT.Copy,
                               scale=to_last[0:META, 0:1]).then_inc(sem("k dec"), 1)
                for c in range(2):
                    act.activation(k_dec[:, c], bank[3][:, c * P:(c + 1) * P], ACT.Copy,
                                   scale=to_last[:, c + 1:c + 2]).then_inc(sem("k dec"), 1)
                act.wait_ge(sem("v turned"), n)
                act.activation(v_beta_m[:, :], bank[4][0:META, 2 * P:3 * P], ACT.Copy,
                               scale=half_beta[0:META, 0:1]).then_inc(sem("v beta"), 1)
                for c in range(2):
                    act.activation(v_beta[:, c], bank[4][:, c * P:(c + 1) * P], ACT.Copy,
                                   scale=half_beta[:, c + 1:c + 2]).then_inc(sem("v beta"), 1)
                for lv, b in enumerate(LEVELS[1:]):
                    act.wait_ge(sem("prod sum"), (n - 1) * 7 + lv + 2)
                    lo = 0 if b < META else META
                    act.activation(prod[:, lo:], bank[5][:, lo:TOK], ACT.Copy).then_inc(sem("prod"), 1)
                act.wait_ge(sem("v new m sum"), n)
                act.activation(v_new_m[:, :], bank[3][0:META, 0:P], ACT.Copy).then_inc(sem("v new m"), 1)
                act.wait_ge(sem("state sum"), 2 * n - 1)
                act.activation(state[:], bank[3][:, P:2 * P], ACT.Copy).then_inc(sem("state"), 1)
                for c in range(2):
                    act.wait_ge(sem("v new sum"), 2 * n - 1 + c)
                    act.activation(v_new[:], bank[4][:, P:2 * P], ACT.Copy).then_inc(sem("v new"), 1)
                act.wait_ge(sem("gdn o"), 2 * n)
                act.activation(sq[:, :SEQ], bank[6][:, 0:SEQ], ACT.Square).then_inc(sem("length sq"), 1)
                rsqrt("gdn o", n, SEQ, 1.0 / P)
                act.wait_ge(sem("gdn y"), 2 * n)
                act.activation(ya_hi[:, bass.ts(n - 1, 1), :], y_out[:, None, :], ACT.Copy).then_inc(
                    sem("ya hi"), 1)

            def fox_act(n):
                for x, y, w in (("q", fq, SEQ), ("k", fk, TOK)):
                    act.activation(sq[:, :w], y[:, :w], ACT.Square).then_inc(sem("length sq"), 1)
                    rsqrt("fox " + x, n, w, 1.0 / P)
                    if x == "q":
                        act.wait_ge(sem("fox qk unit"), 2 * n - 1)
                act.wait_ge(sem("fox v turned"), n)
                act.activation(f_v[:], bank[3][:, 0:2 * P].rearrange("p (c d) -> p c d", c=2),
                               ACT.Copy).then_inc(sem("fox v"), 1)
                act.activation(f_v_m[:, :], bank[3][0:META, 2 * P:3 * P], ACT.Copy).then_inc(sem("fox v"), 1)
                act.wait_ge(sem("fox max"), 2 * n)
                for t in range(2):
                    act.activation(f_p[:, F_AT[t]:F_AT[t] + FW[t]], f_bias[:, F_AT[t]:F_AT[t] + FW[t]], ACT.Exp,
                                   bias=f_max[:, t:t + 1], accum_out=f_sum[:, t:t + 1]).then_inc(
                                       sem("fox e"), 1)
                act.wait_ge(sem("fox p turned"), n)
                act.activation(f_pt[:], bank[5][:, 0:3 * P], ACT.Copy).then_inc(sem("fox pt"), 1)
                act.activation(f_pt_m[:, :], bank[6][0:META, 0:SEQ], ACT.Copy).then_inc(sem("fox pt"), 1)
                act.wait_ge(sem("fox o"), n)
                act.activation(yb_hi[:, bass.ts(n - 1, 1), :], bank[7][:, None, 0:SEQ],
                               ACT.Copy).then_inc(sem("yb hi"), 1)

            dest = [conv_in[0], conv_in[1], conv_in[2], z_raw, fq, fk, fv]
            with act.Fori(0, HEADS // 2) as i:
                for s in range(2):
                    n = i * 2 + s + 1
                    for j in range(MIX_TILES):
                        sl = s * MB + 2 * j
                        split_hi(act, "mix", sl + 2, i, 2 * MB)
                        split_hi(act, "mix", sl + 3, i, 2 * MB)
                        await_slab(act, "mix", sl + 1, i, 2 * MB)
                        b, _ = tile_no("mix", s * MIX_TILES + j)
                        w = SEQ if j in (3, 4) else TOK
                        o = dest[j][:, 3:] if j < 3 else dest[j][:]
                        act.activation(o, proj[b][:, 0:w], ACT.Copy).then_inc(tile_free[b], 1)
                    gdn_act(n)
                    fox_act(n)

            def ahead(phase, n, i=None, per=0):
                split_hi(act, phase, n, i, per)
                split_hi(act, phase, n + 1, i, per)

            with act.Fori(0, KT) as i:
                for j in range(MERGE_TILES):
                    ahead("merge", 2 * j + 2, i, 8)
                    if j < 2:
                        await_slab(act, "merge", 2 * j + 1, i, 8)
                        b, _ = tile_no("merge", j)
                        act.activation((sig_a, sig_b)[j][:], proj[b][:, 0:SEQ], ACT.Tanh,
                                       scale=0.5).then_inc(tile_free[b], 1)
                act.wait_ge(sem("mix v"), i + 1)
                act.activation(mx_hi[:, bass.ts(i, 1), :], mix_v[:, None, :], ACT.Copy,
                               scale=0.5).then_inc(sem("mix hi"), 1)

            def matrix(phase):
                with act.Fori(0, KT // 2) as i:
                    for s in range(2):
                        ahead(phase, 2 * s + 2, i, 4)

            matrix("out")
            act.preload_act_table_set("natural_log_exp_and_others")
            await_tiles_out(act, "up0")
            norm_act(act, 1, h, SEQ, 1)
            for q in range(QUARTERS):
                with act.Fori(0, KT // 2) as i:
                    for s in range(2):
                        ahead(f"up{q}", 2 * s + 2, i, 4)
                        await_slab(act, f"up{q}", 2 * s + 1, i, 4)
                        b, _ = tile_no(f"up{q}", s)
                        act.activation(relu_t[:, s], proj[b][:, 0:SEQ], ACT.Relu).then_inc(tile_free[b], 1)
                        act.wait_ge(sem("hidden v"), i * 2 + (q * KT + s + 1))
                        act.activation(ya_hi[:, bass.ts(i * 2 + s, 1), :], hid_v[:, s, None, :],
                                       ACT.Copy).then_inc(sem("hidden hi"), 1)
                matrix(f"down{q}")
            await_tiles_out(act, "mla_in")
            norm_act(act, 2, h, SEQ, None)
            norm_act(act, 3, h, SEQ, 2)
            for t in range(MLA_IN_TILES):
                ahead("mla_in", 2 * t + 2)
                await_slab(act, "mla_in", 2 * t + 1)
                b, _ = tile_no("mla_in", t)
                act.activation(c_raw[:, t] if t < 2 * RT else k_rope[:], proj[b][:, 0:SEQ],
                               ACT.Copy).then_inc(tile_free[b], 1)
            await_tiles_out(act, "mla")
            for g in range(2):
                for k in range(RT):
                    if g:
                        act.wait_ge(sem("c sum"), k + 1)
                    act.activation(norm_sq[:, k, :SEQ], c_raw[:, g * RT + k], ACT.Square).then_inc(sem("c sq"), 1)
                if g:
                    act.wait_ge(sem("c v"), RT)
                act.wait_ge(sem("c sum"), (g + 1) * RT)
                act.activation(norm_ln[:, :SEQ], bank[2][:, :SEQ], ACT.Ln, scale=1.0 / MLA_RANK,
                               bias=const("eps")).then_inc(sem("c ln"), 1)
                act.wait_ge(sem("c ln"), g + 1)
                act.activation(norm_rs[:, :SEQ], norm_ln[:, :SEQ], ACT.Exp, scale=-0.5).then_inc(sem("c rs"), 1)
                for k in range(RT):
                    act.wait_ge(sem("c v"), g * RT + k + 1)
                    act.activation(c_hi[:, g * RT + k], c_raw[:, g * RT + k], ACT.Copy).then_inc(sem("c hi"), 1)
            for n in range(4):
                act.wait_ge(sem("angle reduced"), n + 1)
                act.activation(cos_sin[("mla", "swa")[n // 2]][1 - n % 2][:], reduced[:],
                               ACT.Sin).then_inc(sem("trig"), 1)

            def softmax_act(tag, c, sinks=None):
                max_at = 2 * c if sinks is None else 2 * HEADS + c
                c = heads_before[tag] + c
                act.wait_ge(sem("head max"), max_at)
                for t in range(2):
                    w = slice(W_AT[t], W_AT[t] + W_W[t])
                    act.activation(probs[:, w], logits[:, w], ACT.Exp, bias=row_max[:, t:t + 1],
                                   accum_out=row_sum[:, t:t + 1]).then_inc(sem("head e"), 1)
                if sinks is not None:
                    act.activation(row_sink[:], row_max[:], ACT.Exp, bias=sinks).then_inc(sem("head e"), 1)
                act.wait_ge(sem("head p turned"), c)
                act.activation(probs_t[:], bank[3][:, 0:3 * P], ACT.Copy).then_inc(sem("head pt"), 1)

            with act.Fori(0, HEADS // 2) as i:
                for s in range(2):
                    ahead("mla", 2 * s + 2, i, 8)
                    await_slab(act, "mla", 2 * s + 1, i, 8)
                    if s:
                        b, turn = tile_no("mla", 0, i, 8)
                        act.wait_ge(tile_free[b], turn + 2)
                    b, _ = tile_no("mla", s)
                    act.activation(gate_t[:], proj[b][:, 0:SEQ], ACT.Tanh, scale=0.5).then_inc(
                        sem("mla tanh"), 1)
                for j, dst in enumerate((q_m, k_m, v_m)):
                    split_hi(act, "mla", 6 + j, i, 8)
                    for s in range(2):
                        if s:
                            await_slab(act, "mla", 4 + j, i, 8)
                        else:
                            act.wait_ge(sem("mla first half"), i * 3 + j + 1)
                        b, _ = tile_no("mla", 2 + 2 * j + s)
                        act.activation(dst[:, s], proj[b][:, 0:SEQ], ACT.Copy).then_inc(tile_free[b], 1)
                split_hi(act, "mla", 9, i, 8)
                await_slab(act, "mla", 7, i, 8)
                act.activation(q_rope[:], bank[7][:, 0:SEQ], ACT.Copy).then_inc(sem("mla qr"), 1)
                for s in range(2):
                    c = i * 2 + s + 1
                    act.wait_ge(sem("mla v turned"), c)
                    act.activation(v_tok[:], bank[4][:, 0:SEQ].rearrange("p (t d) -> p t d", t=2),
                                   ACT.Copy).then_inc(sem("mla v"), 1)
                    softmax_act("mla", c)
                    act.wait_ge(sem("mla y"), c)
                    act.activation(ya_hi[:, bass.ts(i * 2 + s, 1), :], y_v[:, None, :], ACT.Copy).then_inc(
                        sem("mla hi"), 1)
            matrix("mla_out")
            await_tiles_out(act, "swa_kv")
            act.preload_act_table_set("natural_log_exp_and_others")
            norm_act(act, 4, h, SEQ, 3)
            for t in range(SWA_KV_TILES):
                ahead("swa_kv", 2 * t + 2)
                await_slab(act, "swa_kv", 2 * t + 1)
                b, _ = tile_no("swa_kv", t)
                act.activation(k_s[:, t] if t < 4 else v_raw[:, t - 4], proj[b][:, 0:SEQ],
                               ACT.Copy).then_inc(tile_free[b], 1)
            act.wait_ge(sem("swa v turned"), 1)
            act.activation(v_all[:].rearrange("p t g d -> p (t g d)"), bank[4][:, :],
                           ACT.Copy).then_inc(sem("swa v"), 1)
            with act.Fori(0, 4) as i:
                for j in range(4):
                    n = i * 4 + j + 1
                    ahead("swa", 4 * j + 2, i, 16)
                    await_slab(act, "swa", 4 * j + 1, i, 16)
                    b, _ = tile_no("swa", 2 * j)
                    act.activation(q_s[:], proj[b][:, 0:SEQ], ACT.Copy).then_inc(tile_free[b], 1)
                    ahead("swa", 4 * j + 4, i, 16)
                    await_slab(act, "swa", 4 * j + 3, i, 16)
                    b, _ = tile_no("swa", 2 * j + 1)
                    act.activation(s_th[:], proj[b][:, 0:SEQ], ACT.Tanh, scale=0.5).then_inc(
                        sem("swa tanh"), 1)
                    for s in range(2):
                        softmax_act("swa", i * 8 + j * 2 + s + 1, sink[:, 2 * j + s:2 * j + s + 1])
                    act.wait_ge(sem("swa y"), n)
                    act.activation(ya_hi[:, bass.ts(i * 4 + j, 1), :], s_y[:, None, :], ACT.Copy).then_inc(
                        sem("swa hi"), 1)
            matrix("swa_out")
            act.preload_act_table_set("natural_log_exp_and_others")
            await_tiles_out(act, "end")
            norm_act(act, 5, h, SEQ, None)

        @block.vector
        def _(dve):
            dve.wait_ge(inputs_in, 32)
            dve.memset(tokcol[:], 0.0).then_inc(sem("cleared"), 1)
            for b in (5, 6, 7):
                dve.memset(bank[b][:, 0:META], 0.0).then_inc(sem("cleared"), 1)
            dve.wait_ge(sem("x in"), 16)
            norm_dve(dve, 0, xT, TOK, "mix_norm", 0)
            split_lo(dve, "scalars", 0)
            split_lo(dve, "scalars", 1)
            for x in range(3):
                dve.memset(conv_in[x][:, 0:3], 0.0).then_inc(sem("cleared"), 1)
            split_lo(dve, "scalars", 2)
            split_lo(dve, "scalars", 3)
            await_slab(dve, "scalars", 1)
            b, _ = tile_no("scalars", 0)
            dve.tensor_scalar(sc_x[:], proj[b][:, 0:TOK], vec("bias"), None, ALU.add).then_inc(tile_free[b], 1)
            dve.wait_ge(tile_free[b], 2)
            dve.tensor_scalar(sc_xs[:], sc_x[:], const("sign"), None, ALU.mult).then_inc(sem("sc dve"), 1)
            dve.wait_ge(sem("sc act"), 4)
            dve.scalar_tensor_tensor(out=sc_t[0][:], in0=sc_xs[:], scalar=0.0, in1=sc_t[2][:], op0=ALU.max,
                                     op1=ALU.add).then_inc(sem("sc dve"), 1)
            dve.wait_ge(sem("sc dve"), 2)
            dve.wait_ge(sem("sc act"), 4)
            dve.tensor_scalar(sc_t[1][:], sc_t[0][:], sc_rate[:, 0:1], -1.0, ALU.mult,
                              ALU.mult).then_inc(sem("sc dve"), 1)
            dve.wait_ge(sem("sc dve"), 3)
            dve.tensor_tensor_scan(sc_out[:], const("reset"), sc_t[1][:], 0.0, ALU.mult,
                                   ALU.add).then_inc(sem("scalars"), 1)
            dve.wait_ge(sem("scalars"), 1)
            dve.wait_ge(sem("sc act"), 5)
            dve.tensor_scalar(sc_out[0:HEADS, :], sc_t[3][0:HEADS, :], 0.5, 0.5, ALU.mult,
                              ALU.add).then_inc(sem("scalars"), 1)
            dve.sem_inc(sem("row free"), 1)
            dve.wait_ge(sem("tokcol"), 3)

            def inverse_step(n, lv, lo):
                dve.tensor_tensor(b_step[:, lo:], b_mat[:, lo:], const(f"level{LEVELS[lv]}", lo),
                                  ALU.mult).then_inc(sem("b step"), 1)

            def gdn_dve(n):
                for c, (x, y) in enumerate((("k", kT), ("v", vT), ("q", qT))):
                    tile0 = {"q": 0, "k": HEADS, "v": 2 * HEADS}[x]
                    for tap in (3, 2, 1, 0):
                        w_tap = conv_w[:, bass.ts(n - 1 + tile0, 1), tap]
                        src = conv_in[c][:, tap:tap + TOK]
                        done = n * 12 - 8 + 4 * c - tap
                        if tap == 3:
                            dve.wait_ge(tile_free[TF[c][0]], TF[c][1])
                            dve.tensor_scalar(y[:], src, w_tap, None, ALU.mult).then_inc(sem("conv"), 1)
                        else:
                            dve.wait_ge(sem("conv"), done - 1)
                            dve.scalar_tensor_tensor(out=y[:], in0=src, scalar=w_tap, in1=y[:], op0=ALU.mult,
                                                     op1=ALU.add).then_inc(sem("conv"), 1)
                dve.tensor_copy(col[:], tokcol[:, :, :, bass.ts(n - 1, 1)].rearrange(
                    "p c g r -> p c (g r)")).then_inc(sem("col"), 1)
                for c, (x, y) in enumerate((("k", kT), ("v", vT), ("q", qT))):
                    dve.wait_ge(sem("silu tanh"), n * 4 - 3 + c)
                    dve.scalar_tensor_tensor(out=y[:], in0=gate_th[:], scalar=1.0, in1=y[:], op0=ALU.add,
                                             op1=ALU.mult).then_inc(sem("silu"), 1)
                dve.wait_ge(sem("silu tanh"), n * 4)
                dve.scalar_tensor_tensor(out=z_raw[:], in0=gate_th[:, :SEQ], scalar=1.0, in1=z_raw[:],
                                         op0=ALU.add, op1=ALU.mult).then_inc(sem("silu"), 1)
                dve.wait_ge(sem("row in"), n * 16)
                dve.tensor_tensor(b_step[:], row[:, 1], const("future"), ALU.add).then_inc(sem("g diff"), 1)
                dve.wait_ge(sem("col"), n)
                for t in range(2):
                    dve.scalar_tensor_tensor(out=f_bias[:, F_AT[t]:F_AT[t] + FW[t]], in0=row[:, 2, 0:FW[t]],
                                             scalar=col[:, t + 1, 2:3], in1=const(f"fox{t}"), op0=ALU.subtract,
                                             op1=ALU.subtract, reverse1=True).then_inc(sem("fox bias"), 1)
                dve.wait_ge(sem("cols"), 7 * n)
                dve.scalar_tensor_tensor(out=neg_beta_eg[:], in0=col[:, :, 0], scalar=-1.0, in1=eg_col[:],
                                         op0=ALU.mult, op1=ALU.mult).then_inc(sem("neg beta eg"), 1)
                for x, y, f in (("k", kT, 0.5), ("q", qT, 0.5 * HEAD_SCALE)):
                    dve.wait_ge(sem("length rs"), norm_of_head("gdn " + x, n))
                    dve.scalar_tensor_tensor(out=y[:], in0=y[:], scalar=f, in1=rs_t[:], op0=ALU.mult,
                                             op1=ALU.mult).then_inc(sem(x + " unit"), 1)
                dve.wait_ge(sem("q unit"), n)
                dve.wait_ge(sem("g exp"), n)
                dve.tensor_tensor(q_dec[:], qT[:, META:], g_exp[:, META:], ALU.mult).then_inc(sem("q dec"), 1)
                dve.wait_ge(sem("decay"), 3 * n)
                dve.wait_ge(sem("kk"), n)
                dve.tensor_tensor(b_mat[:], bank[5][:, 0:TOK], decay[:], ALU.mult).then_inc(sem("b mat"), 1)
                dve.wait_ge(sem("b mat"), 2 * n - 1)
                dve.tensor_tensor(b_mat[:], b_mat[:], row[:, 0], ALU.mult).then_inc(sem("b mat"), 1)
                dve.wait_ge(sem("b mat"), 2 * n)
                inverse_step(n, 0, 0)
                dve.wait_ge(sem("qk"), n)
                dve.tensor_tensor(qk[:, META:], bank[6][:, META:TOK], decay[:, META:],
                                  ALU.mult).then_inc(sem("qk decayed"), 1)
                dve.wait_ge(sem("fox bias"), 2 * n)
                dve.sem_inc(sem("row free"), 1)
                for lv, b in enumerate(LEVELS):
                    lo = 0 if b < META else META
                    at = (n - 1) * 7 + lv + 1
                    up = (n - 1) * 13 + 2 * lv
                    if not lv:
                        dve.wait_ge(sem("b step"), at)
                        dve.tensor_tensor(inv_t[:], const("identity"), b_step[:], ALU.subtract).then_inc(
                            sem("inverse"), 1)
                        dve.wait_ge(sem("prod sum"), at)
                        dve.wait_ge(sem("inverse"), up + 1)
                        inverse_step(n, 1, 0)
                        dve.tensor_tensor(inv[:], const("identity"), bank[5][:, 0:TOK],
                                          ALU.subtract).then_inc(sem("inverse"), 1)
                        continue
                    dve.wait_ge(sem("prod sum"), at)
                    if lv + 1 < len(LEVELS):
                        inverse_step(n, lv + 1, 0 if LEVELS[lv + 1] < META else META)
                        dve.wait_ge(sem("step t"), (n - 1) * 6 + lv)
                        dve.tensor_tensor(inv[:, lo:], inv[:, lo:], bank[6][:, lo:TOK],
                                          ALU.subtract).then_inc(sem("inverse"), 1)
                    dve.wait_ge(sem("step t"), (n - 1) * 6 + lv)
                    dve.tensor_tensor(inv_t[:, lo:], inv_t[:, lo:], bank[7][:, lo:TOK],
                                      ALU.subtract).then_inc(sem("inverse"), 1)
                dve.wait_ge(sem("neg beta eg"), n)
                dve.wait_ge(sem("v beta"), 3 * n)
                for c in range(2):
                    dve.wait_ge(sem("k state"), 2 * n - 1 + c)
                    dve.scalar_tensor_tensor(out=rhs[:], in0=bank[4][:, 0:P], scalar=neg_beta_eg[:, c + 1:c + 2],
                                             in1=v_beta[:, c], op0=ALU.mult, op1=ALU.add).then_inc(
                                                 sem("rhs"), 1)
                    if c == 0:
                        dve.wait_ge(sem("state sum"), 2 * n)
                        dve.wait_ge(sem("state"), 2 * n - 1)
                        dve.scalar_tensor_tensor(out=state[:], in0=state[:], scalar=eg_last[:, 0:1],
                                                 in1=bank[3][:, P:2 * P], op0=ALU.mult,
                                                 op1=ALU.add).then_inc(sem("state"), 1)
                dve.wait_ge(sem("length rs"), norm_of_head("gdn o", n))
                dve.scalar_tensor_tensor(out=y_out[:], in0=bank[6][:, 0:SEQ], scalar=vec("gdn_norm"),
                                         in1=rs_t[:, :SEQ], op0=ALU.mult, op1=ALU.mult).then_inc(
                                             sem("gdn y"), 1)
                dve.wait_ge(sem("gdn y"), 2 * n - 1)
                dve.wait_ge(sem("silu"), n * 4)
                dve.scalar_tensor_tensor(out=y_out[:], in0=y_out[:], scalar=0.5, in1=z_raw[:], op0=ALU.mult,
                                         op1=ALU.mult).then_inc(sem("gdn y"), 1)
                dve.wait_ge(sem("ya hi"), n)
                dve.tensor_tensor(ya_lo[:, bass.ts(n - 1, 1), :], y_out[:, None, :],
                                  ya_hi[:, bass.ts(n - 1, 1), :].bitcast(F32), ALU.subtract).then_inc(
                                      sem("ya lo"), 1)

            def fox_dve(n):
                for x, y, w in (("q", fq, SEQ), ("k", fk, TOK)):
                    dve.wait_ge(sem("length rs"), norm_of_head("fox " + x, n))
                    dve.scalar_tensor_tensor(out=y[:, :w], in0=y[:, :w], scalar=vec("fox_" + x),
                                             in1=rs_t[:, :w], op0=ALU.mult, op1=ALU.mult).then_inc(
                                                 sem("fox qk unit"), 1)
                dve.wait_ge(sem("fox s"), n)
                w = F_AT[1] + FW[1]
                dve.scalar_tensor_tensor(out=f_bias[:], in0=bank[4][:, 0:w], scalar=HEAD_SCALE, in1=f_bias[:],
                                         op0=ALU.mult, op1=ALU.add).then_inc(sem("fox logits"), 1)
                dve.wait_ge(sem("fox logits"), n)
                for t in range(2):
                    dve.tensor_reduce(f_max[:, t:t + 1], f_bias[:, F_AT[t]:F_AT[t] + FW[t]], AX.X, ALU.max,
                                      negate=True).then_inc(sem("fox max"), 1)
                dve.wait_ge(sem("fox e"), 2 * n)
                dve.reciprocal(f_inv[:], f_sum[:]).then_inc(sem("fox inv"), 1)
                dve.wait_ge(sem("fox inv"), n)
                for t in range(2):
                    o = f_p[:, F_AT[t]:F_AT[t] + FW[t]]
                    dve.tensor_scalar(o, o, f_inv[:, t:t + 1], None, ALU.mult).then_inc(sem("fox p"), 1)
                dve.wait_ge(sem("yb hi"), n)
                dve.tensor_tensor(yb_lo[:, bass.ts(n - 1, 1), :], bank[7][:, None, 0:SEQ],
                                  yb_hi[:, bass.ts(n - 1, 1), :].bitcast(F32), ALU.subtract).then_inc(
                                      sem("yb lo"), 1)

            conv_w = vecs[:, VEC_AT["conv"][0]:VEC_AT["conv"][1]].rearrange("p (t k) -> p t k", k=4)
            with dve.Fori(0, HEADS // 2) as i:
                for s in range(2):
                    n = i * 2 + s + 1
                    TF = []
                    for c in range(3):
                        b, turn = tile_no("mix", s * MIX_TILES + c, i, 2 * MIX_TILES)
                        TF.append((b, turn + 2))
                    for j in range(MIX_TILES):
                        sl = s * MB + 2 * j
                        split_lo(dve, "mix", sl + 2, i, 2 * MB)
                        split_lo(dve, "mix", sl + 3, i, 2 * MB)
                    gdn_dve(n)
                    fox_dve(n)

            def ahead(phase, n, i=None, per=0):
                split_lo(dve, phase, n, i, per)
                split_lo(dve, phase, n + 1, i, per)

            def await_tile_out(phase, n, i=None, per=0):
                b, turn = tile_no(phase, n, i, per)
                dve.wait_ge(tile_free[b], turn + 2)

            with dve.Fori(0, KT) as i:
                for j in range(MERGE_TILES):
                    ahead("merge", 2 * j + 2, i, 8)
                    if j >= 2:
                        if j == 2:
                            await_tile_out("merge", 0, i, 4)
                            await_tile_out("merge", 1, i, 4)
                        await_slab(dve, "merge", 2 * j + 1, i, 8)
                        b, _ = tile_no("merge", j)
                        dve.scalar_tensor_tensor(out=(mix_a, mix_b)[j - 2][:], in0=(sig_a, sig_b)[j - 2][:],
                                                 scalar=1.0, in1=proj[b][:, 0:SEQ], op0=ALU.add,
                                                 op1=ALU.mult).then_inc(tile_free[b], 1)
                await_tile_out("merge", 2, i, 4)
                await_tile_out("merge", 3, i, 4)
                dve.tensor_tensor(mix_v[:], mix_a[:], mix_b[:], ALU.add).then_inc(sem("mix v"), 1)
                dve.wait_ge(sem("mix hi"), i + 1)
                dve.scalar_tensor_tensor(out=mx_lo[:, bass.ts(i, 1), :], in0=mix_v[:, None, :], scalar=0.5,
                                         in1=mx_hi[:, bass.ts(i, 1), :].bitcast(F32), op0=ALU.mult,
                                         op1=ALU.subtract).then_inc(sem("mix lo"), 1)

            def residual(phase):
                with dve.Fori(0, KT // 2) as i:
                    for s in range(2):
                        ahead(phase, 2 * s + 2, i, 4)
                        await_slab(dve, phase, 2 * s + 1, i, 4)
                        b, _ = tile_no(phase, s)
                        o = h[:, bass.ts(i * 2 + s, 1), :]
                        dve.tensor_tensor(o, proj[b][:, None, 0:SEQ], o, ALU.add).then_inc(tile_free[b], 1)

            dve.wait_ge(sem("h in"), 16)
            residual("out")
            norm_dve(dve, 1, h, SEQ, "mlp_norm", 1)
            for q in range(QUARTERS):
                with dve.Fori(0, KT // 2) as i:
                    for s in range(2):
                        ahead(f"up{q}", 2 * s + 2, i, 4)
                        await_tile_out(f"up{q}", s, i, 2)
                        dve.tensor_tensor(hid_v[:, s], relu_t[:, s], relu_t[:, s], ALU.mult).then_inc(
                            sem("hidden v"), 1)
                        dve.wait_ge(sem("hidden hi"), i * 2 + (q * KT + s + 1))
                        t = bass.ts(i * 2 + s, 1)
                        dve.tensor_tensor(ya_lo[:, t, :], hid_v[:, s, None, :], ya_hi[:, t, :].bitcast(F32),
                                          ALU.subtract).then_inc(sem("hidden lo"), 1)
                residual(f"down{q}")
            norm_dve(dve, 2, h, SEQ, "final_norm", None)
            norm_dve(dve, 3, h, SEQ, "layer0", 2)
            for t in range(MLA_IN_TILES):
                ahead("mla_in", 2 * t + 2)
            for g in range(2):
                dve.wait_ge(sem("c rs"), g + 1)
                for k in range(RT):
                    o = c_raw[:, g * RT + k]
                    dve.scalar_tensor_tensor(out=o, in0=o, scalar=vec(("mla_q", "mla_kv")[g], k),
                                             in1=norm_rs[:, :SEQ], op0=ALU.mult, op1=ALU.mult).then_inc(
                                                 sem("c v"), 1)
                for k in range(RT):
                    dve.wait_ge(sem("c hi"), g * RT + k + 1)
                    dve.tensor_tensor(c_lo[:, g * RT + k], c_raw[:, g * RT + k],
                                      c_hi[:, g * RT + k].bitcast(F32), ALU.subtract).then_inc(sem("c lo"), 1)

            steps = [0]

            def step(ins):
                steps[0] += 1
                ins.then_inc(sem("angle step"), 1)
                dve.wait_ge(sem("angle step"), steps[0])

            dve.wait_ge(sem("positions in"), 16)
            step(dve.tensor_copy(pos_f[:], pos_i[:]))
            for n in range(4):
                shift = n % 2
                if n % 2 == 0:
                    step(dve.tensor_scalar(angle[:], pos_f[:], const("freq_" + ("mla", "swa")[n // 2]), None,
                                           ALU.mult))
                step(dve.tensor_scalar(turns[:], angle[:], float(1 / (2 * np.pi)), 0.25 * shift, ALU.mult,
                                       ALU.add))
                step(dve.tensor_scalar(turns[:], turns[:], ROUND, None, ALU.add))
                step(dve.tensor_scalar(turns[:], turns[:], ROUND, None, ALU.subtract))
                if n:
                    dve.wait_ge(sem("trig"), n)
                step(dve.scalar_tensor_tensor(out=reduced[:], in0=turns[:], scalar=-TURN_HI, in1=angle[:],
                                              op0=ALU.mult, op1=ALU.add))
                step(dve.scalar_tensor_tensor(out=reduced[:], in0=turns[:], scalar=-TURN_LO, in1=reduced[:],
                                              op0=ALU.mult, op1=ALU.add))
                step(dve.tensor_scalar(reduced[:], reduced[:], float(np.pi / 2 * shift), None, ALU.add))
                dve.tensor_scalar(reduced[:], reduced[:], PI_BELOW, -PI_BELOW, ALU.min, ALU.max).then_inc(
                    sem("angle reduced"), 1)

            def rope(n, x, kind):
                cos, sin = cos_sin[kind]
                dve.wait_ge(sem("turned half"), n)
                dve.tensor_tensor(rope_a[:], x, cos[:], ALU.mult).then_inc(sem("rotation parts"), 1)
                dve.tensor_tensor(rope_b[:], bank[6][:, 0:SEQ], sin[:], ALU.mult).then_inc(sem("rotation parts"), 1)
                dve.wait_ge(sem("rotation parts"), 2 * n)
                dve.tensor_tensor(x, rope_a[:], rope_b[:], ALU.add).then_inc(sem("rotated"), 1)

            dve.wait_ge(sem("trig"), 4)
            rope(1, k_rope[:], "mla")

            def softmax_dve(tag, c, scale, mask, sinks=None):
                e_at = 2 * c if sinks is None else 2 * HEADS + 3 * c
                key_max_at = 2 * c
                c = heads_before[tag] + c
                dve.wait_ge(sem("head s"), c)
                dve.scalar_tensor_tensor(out=logits[:], in0=bank[2][:, 0:3 * P], scalar=scale, in1=const(mask),
                                         op0=ALU.mult, op1=ALU.add).then_inc(sem("head logits"), 1)
                dve.wait_ge(sem("head logits"), c)
                top_ = sem("head max" if sinks is None else "head key max")
                for t in range(2):
                    dve.tensor_reduce(row_max[:, t:t + 1], logits[:, W_AT[t]:W_AT[t] + W_W[t]], AX.X, ALU.max,
                                      negate=True).then_inc(top_, 1)
                if sinks is None:
                    dve.wait_ge(sem("head e"), e_at)
                else:
                    dve.wait_ge(top_, key_max_at)
                    dve.tensor_scalar(row_max[:], row_max[:], sinks, None, ALU.min).then_inc(sem("head max"), 1)
                    dve.wait_ge(sem("head e"), e_at)
                    dve.tensor_tensor(row_sum[:], row_sum[:], row_sink[:], ALU.add).then_inc(
                        sem("head sum"), 1)
                    dve.wait_ge(sem("head sum"), c - HEADS)
                dve.reciprocal(row_inv[:], row_sum[:]).then_inc(sem("head inv"), 1)
                dve.wait_ge(sem("head inv"), c)
                for t in range(2):
                    o = probs[:, W_AT[t]:W_AT[t] + W_W[t]]
                    dve.tensor_scalar(o, o, row_inv[:, t:t + 1], None, ALU.mult).then_inc(sem("head p"), 1)

            dve.sem_inc(sem("mla qr free"), 1)
            with dve.Fori(0, HEADS // 2) as i:
                for s in range(2):
                    ahead("mla", 2 * s + 2, i, 8)
                    dve.wait_ge(sem("mla tanh"), i * 2 + s + 1)
                    b, _ = tile_no("mla", s)
                    dve.scalar_tensor_tensor(out=gate_s[:, s], in0=gate_t[:], scalar=1.0, in1=proj[b][:, 0:SEQ],
                                             op0=ALU.add, op1=ALU.mult).then_inc(tile_free[b], 1)
                for j in range(3):
                    split_lo(dve, "mla", 6 + j, i, 8)
                split_lo(dve, "mla", 9, i, 8)
                rope(i + 2, q_rope[:], "mla")
                dve.sem_inc(sem("mla qr free"), 1)
                for s in range(2):
                    c = i * 2 + s + 1
                    softmax_dve("mla", c, MLA_SCALE, "causal")
                    dve.wait_ge(sem("head o"), c)
                    if s == 0:
                        await_tile_out("mla", 0, i, 8)
                        await_tile_out("mla", 1, i, 8)
                    dve.scalar_tensor_tensor(out=y_v[:], in0=bank[5][:, 0:SEQ], scalar=0.5, in1=gate_s[:, s],
                                             op0=ALU.mult, op1=ALU.mult).then_inc(sem("mla y"), 1)
                    dve.wait_ge(sem("mla hi"), c)
                    t = bass.ts(i * 2 + s, 1)
                    dve.tensor_tensor(ya_lo[:, t, :], y_v[:, None, :], ya_hi[:, t, :].bitcast(F32),
                                      ALU.subtract).then_inc(sem("mla lo"), 1)
            residual("mla_out")
            norm_dve(dve, 4, h, SEQ, "layer1", 3)
            for t in range(SWA_KV_TILES):
                ahead("swa_kv", 2 * t + 2)
            for t in range(4):
                rope(t + SWA_K_TURNS, k_s[:, t], "swa")
            dve.wait_ge(sem("rotated"), SWA_K_TURNS + 3)
            dve.wait_ge(sem("swa v"), 1)
            sink_at = VEC_AT["sinks"][0]
            with dve.Fori(0, 4) as i:
                dve.tensor_copy(k_own[:, None, :], k_s[:, bass.ts(i, 1), :]).then_inc(sem("swa own"), 1)
                dve.tensor_copy(v_own[:, :, None, :], v_all[:, :, bass.ts(i, 1), :]).then_inc(sem("swa own"), 1)
                dve.tensor_copy(sink[:], vecs[:, bass.ds(i * 8 + sink_at, 8)]).then_inc(sem("swa own"), 1)
                dve.tensor_scalar(neg_sink[:], vecs[:, bass.ds(i * 8 + sink_at, 8)], -1.0, None,
                                  ALU.mult).then_inc(sem("swa own"), 1)
                dve.wait_ge(sem("swa own"), i * 4 + 4)
                for j in range(4):
                    n = i * 4 + j + 1
                    ahead("swa", 4 * j + 2, i, 16)
                    ahead("swa", 4 * j + 4, i, 16)
                    dve.wait_ge(sem("swa tanh"), n)
                    b, _ = tile_no("swa", 2 * j + 1)
                    dve.scalar_tensor_tensor(out=s_gate[:], in0=s_th[:], scalar=1.0, in1=proj[b][:, 0:SEQ],
                                             op0=ALU.add, op1=ALU.mult).then_inc(tile_free[b], 1)
                    rope(n + SWA_Q_TURNS, q_s[:], "swa")
                    for s in range(2):
                        softmax_dve("swa", i * 8 + j * 2 + s + 1, SWA_SCALE, "window",
                                    neg_sink[:, 2 * j + s:2 * j + s + 1])
                    dve.wait_ge(sem("head o"), 2 * n + HEADS)
                    await_tile_out("swa", 2 * j + 1, i, 8)
                    dve.scalar_tensor_tensor(out=s_y[:], in0=bank[5][:, 0:SEQ], scalar=0.5, in1=s_gate[:],
                                             op0=ALU.mult, op1=ALU.mult).then_inc(sem("swa y"), 1)
                    dve.wait_ge(sem("swa hi"), n)
                    t = bass.ts(i * 4 + j, 1)
                    dve.tensor_tensor(ya_lo[:, t, :], s_y[:, None, :], ya_hi[:, t, :].bitcast(F32),
                                      ALU.subtract).then_inc(sem("swa lo"), 1)
            residual("swa_out")
            norm_dve(dve, 5, h, SEQ, "final2", None)


def slabs_of(w):
    k, n = w.shape
    return w.reshape(k // (HALF_KT * P), HALF_KT, P, n // P, P).transpose(3, 0, 2, 1, 4)


def lay_out(i):
    f32 = np.float32
    stream = np.zeros((STREAM, P, HALF_KT, P), f32)
    pos = [0]

    def put(slabs):
        slabs = slabs.reshape(-1, P, HALF_KT, P)
        stream[pos[0]:pos[0] + len(slabs)] = slabs
        pos[0] += len(slabs)

    w_in = np.asarray(i["w_in"])[0]
    edges = np.cumsum([0, 6144, 2048, 16, 16, 6144, 16, 2048, 2048])
    qkv_a, z_a, b_a, a_a, qkv_b, f_b, gate_a, gate_b = (w_in[:, a:b] for a, b in zip(edges[:-1], edges[1:]))
    scalars = np.zeros((D, P), f32)
    scalars[:, 0:16], scalars[:, 32:48], scalars[:, 64:80] = b_a, a_a, f_b
    put(slabs_of(scalars))
    qa, ka, va = (slabs_of(qkv_a[:, j * D:(j + 1) * D]) for j in range(3))
    qb, kb, vb = (slabs_of(qkv_b[:, j * D:(j + 1) * D]) for j in range(3))
    put(np.stack([ka, va, qa, slabs_of(z_a), qb, kb, vb], axis=1))
    put(np.stack([slabs_of(gate_a), slabs_of(gate_b), slabs_of(np.asarray(i["w_o_gdn"])[0]),
                  slabs_of(np.asarray(i["w_o_fox"])[0])], axis=1))
    put(slabs_of(np.asarray(i["w_out"])[0]))
    up, down = np.asarray(i["w_up"])[0], np.asarray(i["w_down"])[0]
    for q in range(QUARTERS):
        put(slabs_of(up[:, q * D:(q + 1) * D]))
        put(slabs_of(down[q * D:(q + 1) * D]))
    mla = np.asarray(i["mla_w_in_2"])[0]
    c_q, c_kv, k_r, gate = (mla[:, a:b] for a, b in ((0, 512), (512, 1024), (1024, 1088), (1088, 3136)))
    put(slabs_of(np.concatenate([c_q, c_kv, k_r, k_r], axis=1)))

    def quarters(w):
        return w.reshape(RT, P, -1, P).transpose(2, 1, 0, 3)

    uq = np.asarray(i["mla_w_uq_2"])[0].reshape(MLA_RANK, HEADS, 192)
    ukv = np.asarray(i["mla_w_ukv_2"])[0].reshape(MLA_RANK, HEADS, 256)
    qn = quarters(uq[:, :, :P].reshape(MLA_RANK, -1))
    qr = quarters(uq[:, :, P:].reshape(MLA_RANK, -1))
    kn = quarters(ukv[:, :, :P].reshape(MLA_RANK, -1))
    vv = quarters(ukv[:, :, P:].reshape(MLA_RANK, -1))
    gates = slabs_of(gate)
    for pair in range(HEADS // 2):
        a, b = 2 * pair, 2 * pair + 1
        put(gates[a:b + 1])
        for x in (qn, kn, vv):
            put(np.concatenate([x[a], x[b]], axis=1))
        put(np.concatenate([qr[pair], np.zeros_like(qr[pair])], axis=1))
    put(slabs_of(np.asarray(i["mla_w_out_2"])[0]))
    swa = np.asarray(i["swa_w_in_2"])[0]
    q, k, v, gate = (swa[:, a:b] for a, b in ((0, 2048), (2048, 2304), (2304, 2560), (2560, 4608)))
    k = k.reshape(D, 4, 64)
    put(slabs_of(np.concatenate([k, k], axis=2).reshape(D, 512)))
    put(slabs_of(v))
    put(np.stack([slabs_of(q), slabs_of(gate)], axis=1))
    put(slabs_of(np.asarray(i["swa_w_out_2"])[0]))

    vecs = np.zeros((P, VEC_N), f32)

    def vec(name, a):
        lo, hi = VEC_AT[name]
        vecs[:a.shape[0], lo:hi] = a

    def column(a):
        return np.asarray(a).reshape(-1, P).T

    vec("mix_norm", column(i["mix_norm_g"]))
    vec("mlp_norm", column(i["mlp_norm_g"]))
    vec("final_norm", column(i["final_norm_g"]))
    vec("layer0", column(i["layer_norm_2"][0]))
    vec("layer1", column(i["layer_norm_2"][1]))
    vec("final2", column(i["final_norm_2"]))
    vec("conv", np.asarray(i["conv_w"])[0].reshape(4, 48, P).transpose(2, 1, 0).reshape(P, -1))
    vec("gdn_norm", column(i["gdn_norm_g"]))
    vec("fox_q", column(i["fox_q_norm_g"]))
    vec("fox_k", column(i["fox_k_norm_g"]))
    bias, a_log = np.zeros((P, 1), f32), np.zeros((P, 1), f32)
    bias[32:48, 0], bias[64:80, 0] = np.asarray(i["dt_bias"])[0], np.asarray(i["fox_f_bias"])[0]
    a_log[32:48, 0] = np.asarray(i["a_log"])[0]
    vec("bias", bias)
    vec("a_log", a_log)
    vec("mla_q", column(i["mla_q_norm_2"]))
    vec("mla_kv", column(i["mla_kv_norm_2"]))
    vec("sinks", np.broadcast_to(np.asarray(i["swa_sinks_2"])[0], (P, 32)))
    x = np.concatenate([np.asarray(i["meta_tokens"]), np.asarray(i["x"])[0]], axis=0)
    xT = x.T.reshape(KT, P, TOK).transpose(1, 0, 2)
    return {"stream": stream.reshape(STREAM, P, SLAB), "consts": CONST, "vecs": vecs,
            "xT": np.ascontiguousarray(xT), "positions": np.asarray(i["positions_2"])}


def kernel(**inputs):
    import concourse.bacc as bacc
    from concourse.bass_utils import run_bass_kernel_spmd

    nc = bacc.Bacc("TRN2", target_bir_lowering=False, num_devices=1)
    arrays = lay_out(inputs)
    args = {k: nc.dram_tensor(f"in_{k}", a.shape, mybir.dt.from_np(a.dtype), kind="ExternalInput").ap()
            for k, a in arrays.items()}
    rows = nc.dram_tensor("rows", (P, TOK), F32, kind="Internal").ap()
    out = nc.dram_tensor("out_dram", (P, KT, SEQ), F32, kind="ExternalOutput").ap()
    program(nc, args["stream"], args["consts"], args["vecs"], args["xT"], args["positions"], rows, out)
    r = run_bass_kernel_spmd(nc, [{f"in_{k}": a for k, a in arrays.items()}], core_ids=[0])
    y = r.results[0]["out_dram"]
    return np.ascontiguousarray(y.transpose(1, 0, 2).reshape(1, D, SEQ).transpose(0, 2, 1))
```

```python
from contextlib import ExitStack

import numpy as np

import concourse.bass as bass
from concourse import mybir

P = 128
D = 2048
KT = D // P
META, SEQ = 16, 256
TOK = META + SEQ
HEADS = 16
FF = 4 * D
EPS = 1e-6
HALF_KT = 8
SLAB = HALF_KT * P
RING = 4
MLA_RANK = 512
RT = MLA_RANK // P
ROPE_THETA = 500000.0
NEG = -1e30
HEAD_SCALE = float(P) ** -0.5
MLA_SCALE = float(P + 64) ** -0.5
SWA_SCALE = 64.0 ** -0.5
WINDOW = 128
ROUND = 1.5 * 2.0 ** 23
TURN_HI = 6.28125
TURN_LO = float(2 * np.pi - 6.28125)
PI_BELOW = 3.1415925
LEVELS = (1, 2, 4, 8, 16, 32, 64)

F32 = mybir.dt.float32
F32R = mybir.dt.float32r
I32 = mybir.dt.int32
ALU = mybir.AluOpType
ACT = mybir.ActivationFunctionType
AX = mybir.AxisListType

CHUNKS = ((0, META), (META, P), (META + P, P))
MAIN = CHUNKS[1:]
MAIN_FIRST = MAIN + CHUNKS[:1]

SCALARS_SLABS = 2
MIX_TILES = 7
MERGE_TILES = 4
QUARTERS = 4
MLA_IN_TILES = 9
MLA_PAIR_TILES = 8
SWA_KV_TILES = 6


def phase_table():
    phases = [("scalars", 2, 1), ("mix", HEADS * 2 * MIX_TILES, HEADS * MIX_TILES),
              ("merge", KT * 2 * MERGE_TILES, KT * MERGE_TILES), ("out", KT * 2, KT)]
    for q in range(QUARTERS):
        phases += [(f"up{q}", KT * 2, KT), (f"down{q}", KT * 2, KT)]
    phases += [("mla_in", 2 * MLA_IN_TILES, MLA_IN_TILES), ("mla", 8 * 8, 8 * MLA_PAIR_TILES),
               ("mla_out", KT * 2, KT), ("swa_kv", 2 * SWA_KV_TILES, SWA_KV_TILES),
               ("swa", KT * 4, KT * 2), ("swa_out", KT * 2, KT)]
    table, slab, tile = {}, 0, 0
    for name, slabs, tiles in phases:
        table[name] = (slab, tile)
        slab, tile = slab + slabs, tile + tiles
    table["end"] = (slab, tile)
    return table, slab


TABLE, SLABS = phase_table()
STREAM = -(-(SLABS + 2) // RING) * RING


def constants():
    at, parts, n = {}, [], 0

    def add(name, a):
        nonlocal n
        full = np.zeros((P, a.shape[1]), np.float32)
        full[:a.shape[0]] = a
        at[name] = (n, n + a.shape[1])
        parts.append(full)
        n += a.shape[1]

    def blocks(square, below=0.0):
        meta = np.full((P, META), below, np.float32)
        meta[:META] = square[:META, :META]
        return np.concatenate([meta, square, square], axis=1)

    j, i = np.arange(P)[:, None], np.arange(P)[None, :]
    add("identity", blocks(np.eye(P, dtype=np.float32)))
    add("ones", np.ones((P, P), np.float32))
    add("future", blocks(np.where(j > i, np.float32(NEG), np.float32(0)), NEG))
    for b in LEVELS:
        step = (j // (2 * b) == i // (2 * b)) & ((i // b) % 2 == 1) & ((j // b) % 2 == 0)
        add(f"level{b}", blocks(step.astype(np.float32)))
    qi, key = np.arange(P)[:, None], np.arange(TOK)[None, :]
    add("fox0", np.where(key[:, :META + P] <= qi + META, np.float32(0), np.float32(NEG)))
    add("fox1", np.where(key <= qi + META + P, np.float32(0), np.float32(NEG)))
    key = np.arange(SEQ)[None, :]
    first = np.where(key[:, :P] <= qi, np.float32(0), np.float32(NEG))
    add("causal", np.concatenate([first, np.where(key <= qi + P, np.float32(0), np.float32(NEG))], axis=1))
    near = (key <= qi + P) & (qi + P - key < WINDOW)
    add("window", np.concatenate([first, np.where(near, np.float32(0), np.float32(NEG))], axis=1))

    def turn(dim, rot):
        m = np.zeros((P, P), np.float32)
        for r in range(P):
            o, h = r % dim, rot // 2
            if o < h:
                m[r + h, r] = -1
            elif o < rot:
                m[r - h, r] = 1
        return m

    add("turn_mla", turn(64, 64))
    add("turn_swa", turn(64, 16))

    def freq(rot):
        o = np.arange(P) % 64
        inv = np.float32(ROPE_THETA) ** (-(np.arange(0, rot, 2, dtype=np.float32)) / np.float32(rot))
        return np.where(o < rot, inv.astype(np.float32)[o % (rot // 2)], 0).astype(np.float32)[:, None]

    add("freq_mla", freq(64))
    add("freq_swa", freq(16))
    sign = np.ones((P, 1), np.float32)
    sign[64:80] = -1
    add("sign", sign)
    add("eps", np.full((P, 1), EPS, np.float32))
    reset = np.ones((P, TOK), np.float32)
    for start, _ in CHUNKS:
        reset[32:48, start] = 0
    add("reset", reset)
    return np.concatenate(parts, axis=1), at


CONST, CONST_AT = constants()

VEC_AT, VEC_N = {}, 0
for _name, _n in (("mix_norm", KT), ("mlp_norm", KT), ("final_norm", KT), ("layer0", KT), ("layer1", KT),
                  ("final2", KT), ("conv", 48 * 4), ("gdn_norm", 1), ("fox_q", 1), ("fox_k", 1),
                  ("bias", 1), ("a_log", 1), ("mla_q", RT), ("mla_kv", RT), ("sinks", 32)):
    VEC_AT[_name] = (VEC_N, VEC_N + _n)
    VEC_N += _n


def program(nc, stream, consts_in, vecs_in, xT_in, positions_in, rows, out):
    with ExitStack() as ctx:
        cursor = [-(-nc.sbuf_base // 64) * 64]

        def place(name, shape, dt=F32, at=None):
            size = int(np.prod(shape[1:])) * 4
            where = cursor[0] if at is None else at
            if at is None:
                cursor[0] += -(-size // 64) * 64
            return nc.alloc_sbuf_tensor_at(name, list(shape), dt, offset=where)

        def region(size):
            start = cursor[0]
            cursor[0] += size
            return start

        raw = place("raw", [P, RING, SLAB])
        w_hi = place("w_hi", [P, RING, SLAB], F32R)
        w_lo = place("w_lo", [P, RING, SLAB], F32R)
        u_hi = place("u_hi", [P, KT, TOK], F32R)
        u_lo = place("u_lo", [P, KT, TOK], F32R)
        ya_at = region(2 * KT * SEQ * 4)
        ya_hi = place("ya_hi", [P, KT, SEQ], F32R, ya_at)
        ya_lo = place("ya_lo", [P, KT, SEQ], F32R, ya_at + KT * SEQ * 4)
        yb_at = region(2 * KT * SEQ * 4)
        yb_hi = place("yb_hi", [P, KT, SEQ], F32R, yb_at)
        yb_lo = place("yb_lo", [P, KT, SEQ], F32R, yb_at + KT * SEQ * 4)
        h = place("h", [P, KT, SEQ], F32, yb_at)
        mx_at = region(2 * KT * SEQ * 4)
        mx_hi = place("mx_hi", [P, KT, SEQ], F32R, mx_at)
        mx_lo = place("mx_lo", [P, KT, SEQ], F32R, mx_at + KT * SEQ * 4)
        xT = place("xT", [P, KT, TOK], F32, mx_at)
        consts = place("consts", [P, CONST.shape[1]])
        vecs = place("vecs", [P, VEC_N])
        tokcol = place("tokcol", [P, 3, 4, 32])
        top = cursor[0]

        def const(name, lo=0, hi=None, rows_=P):
            a, b = CONST_AT[name]
            return consts[0:rows_, a + lo:(b if hi is None else a + hi)]

        def vec(name, k=0, n=1):
            a = VEC_AT[name][0] + k
            return vecs[:, a:a + n]

        class Temps:

            def __init__(self, tag, spans):
                self.tag, self.spans = tag, [list(s) for s in spans]

            def __call__(self, name, shape, dt=F32):
                size = -(-int(np.prod(shape[1:])) * 4 // 64) * 64
                for s in self.spans:
                    if s[0] + size <= s[1]:
                        s[0] += size
                        return nc.alloc_sbuf_tensor_at(f"{self.tag}_{name}", list(shape), dt, offset=s[0] - size)
                raise AssertionError((self.tag, name))

        mx_span = (mx_at, mx_at + 2 * KT * SEQ * 4)
        end_span = (top, nc.sbuf_usable_end // 64 * 64)

        bank = [ctx.enter_context(nc.psum_tensor(f"bank{b}", [P, 512], F32)) for b in range(8)]
        proj = bank[0:2]

        named = {}

        def sem(name):
            if name not in named:
                named[name] = ctx.enter_context(nc.semaphore(name.replace(" ", "_")))
            return named[name]

        landed = [sem(f"slab {r} landed") for r in range(RING)]
        hi_ready, lo_ready, slab_used = sem("w_hi ready"), sem("w_lo ready"), sem("slab used")
        inputs_in = sem("inputs in")
        tile_free = [sem(f"proj {b} free") for b in range(2)]

        def slab_no(phase, n, i=None, per=0):
            m = TABLE[phase][0] + n
            assert per % RING == 0
            if i is None:
                return m, m % RING, m // RING
            return m + i * per, m % RING, m // RING + i * (per // RING)

        def split_hi(act, phase, n, i=None, per=0):
            m, slot, turn = slab_no(phase, n, i, per)
            act.wait_ge(landed[slot], (turn + 1) * 16)
            act.wait_ge(slab_used, m + 1)
            act.activation(w_hi[:, slot], raw[:, slot], ACT.Copy).then_inc(hi_ready, 1)

        def split_lo(dve, phase, n, i=None, per=0):
            m, slot, _ = slab_no(phase, n, i, per)
            dve.wait_ge(hi_ready, m + 1)
            dve.tensor_tensor(w_lo[:, slot], raw[:, slot], w_hi[:, slot].bitcast(F32),
                              ALU.subtract).then_inc(lo_ready, 1)

        def tile_no(phase, n, i=None, per=0):
            t = TABLE[phase][1] + n
            assert per % 2 == 0
            if i is None:
                return t % 2, t // 2
            return t % 2, t // 2 + i * (per // 2)

        def await_slab(eng, phase, n, i=None, per=0):
            eng.wait_ge(slab_used, slab_no(phase, n, i, per)[0] + 1 + RING)

        def await_tiles_out(eng, phase):
            t = TABLE[phase][1]
            for b in range(2):
                eng.wait_ge(tile_free[b], (t + 1 - b) // 2 + 1)

        def products(pe, phase, slab, o, x, first, last, i=None, per=0):
            m, slot, _ = slab_no(phase, slab, i, per)
            pe.wait_ge(lo_ready, m + 1)
            for k in range(HALF_KT):
                a, b = w_hi[:, slot, k * P:(k + 1) * P], w_lo[:, slot, k * P:(k + 1) * P]
                x_hi, x_lo = x(k if first else HALF_KT + k)
                pe.matmul(o, a, x_hi, start=first and k == 0, stop=False)
                pe.matmul(o, a, x_lo, start=False, stop=False)
                mm = pe.matmul(o, b, x_hi, start=False, stop=last and k == HALF_KT - 1)
            mm.then_inc(slab_used, 1)

        def full_tile(pe, phase, n, x, width, slab, i=None, slabs_per=0, tiles_per=0):
            b, turn = tile_no(phase, n, i, tiles_per)
            pe.wait_ge(tile_free[b], turn + 1)
            o = proj[b][:, 0:width]
            products(pe, phase, slab, o, x, True, False, i, slabs_per)
            products(pe, phase, slab + 1, o, x, False, True, i, slabs_per)

        def u_all(k):
            return u_hi[:, k, :], u_lo[:, k, :]

        def u_seq(k):
            return u_hi[:, k, META:], u_lo[:, k, META:]

        def ya(k):
            return ya_hi[:, k], ya_lo[:, k]

        def yb(k):
            return yb_hi[:, k], yb_lo[:, k]

        def mx(k):
            return mx_hi[:, k], mx_lo[:, k]

        norm_t = Temps("norm", [(ya_at, ya_at + 2 * KT * SEQ * 4)])
        norm_sq, norm_v = norm_t("sq", [P, 4, TOK]), norm_t("v", [P, 4, TOK])
        norm_ln, norm_rs = norm_t("ln", [P, TOK]), norm_t("rs", [P, TOK])

        def norm_act(act, nu, src, width, split):
            w = width
            if nu:
                act.wait_ge(sem("norm done"), nu)
            for k in range(KT):
                if k >= 4:
                    act.wait_ge(sem("norm sq used"), nu * KT + k - 3)
                act.activation(norm_sq[:, k % 4, :w], src[:, k, :w], ACT.Square).then_inc(sem("norm sq"), 1)
            act.wait_ge(sem("norm sq used"), (nu + 1) * KT)
            act.activation(norm_ln[:, :w], bank[2][:, :w], ACT.Ln, scale=1.0 / D,
                           bias=const("eps")).then_inc(sem("norm ln"), 1)
            act.wait_ge(sem("norm ln"), nu + 1)
            act.activation(norm_rs[:, :w], norm_ln[:, :w], ACT.Exp, scale=-0.5).then_inc(sem("norm rs"), 1)
            if split is not None:
                for k in range(KT):
                    act.wait_ge(sem("norm v"), split * KT + k + 1)
                    act.activation(u_hi[:, k, TOK - w:], norm_v[:, k % 4, :w],
                                   ACT.Copy).then_inc(sem("norm hi"), 1)

        def norm_pe(pe, nu, width):
            for k in range(KT):
                pe.wait_ge(sem("norm sq"), nu * KT + k + 1)
                pe.matmul(bank[2][:, :width], const("ones"), norm_sq[:, k % 4, :width], start=k == 0,
                          stop=k == KT - 1).then_inc(sem("norm sq used"), 1)

        def norm_dve(dve, nu, src, width, gain, split):
            w = width
            dve.wait_ge(sem("norm rs"), nu + 1)
            if split is None:
                for k in range(KT):
                    ins = dve.scalar_tensor_tensor(out=src[:, k, :w], in0=src[:, k, :w], scalar=vec(gain, k),
                                                   in1=norm_rs[:, :w], op0=ALU.mult, op1=ALU.mult)
                    ins.then_inc(sem("norm in place"), 1)
                dve.wait_ge(sem("norm in place"), KT * (1 if nu < 5 else 2))
                dve.sem_inc(sem("norm done"), 1)
                return
            for k in range(KT + 1):
                if k < KT:
                    if k >= 4:
                        dve.wait_ge(sem("norm lo"), split * KT + k - 3)
                    dve.scalar_tensor_tensor(out=norm_v[:, k % 4, :w], in0=src[:, k, :w], scalar=vec(gain, k),
                                             in1=norm_rs[:, :w], op0=ALU.mult,
                                             op1=ALU.mult).then_inc(sem("norm v"), 1)
                if k:
                    dve.wait_ge(sem("norm hi"), split * KT + k)
                    dve.tensor_tensor(u_lo[:, k - 1, TOK - w:], norm_v[:, (k - 1) % 4, :w],
                                      u_hi[:, k - 1, TOK - w:].bitcast(F32), ALU.subtract).then_inc(sem("norm lo"), 1)
            dve.wait_ge(sem("norm lo"), (split + 1) * KT)
            dve.sem_inc(sem("norm done"), 1)

        mt = Temps("mix", [mx_span, end_span])
        conv_in = [mt(f"conv_in_{x}", [P, 3 + TOK]) for x in "kvq"]
        kT, vT, qT = (mt(x, [P, TOK]) for x in ("kT", "vT", "qT"))
        gate_th = mt("th", [P, TOK])
        z_raw, z_silu = mt("z_raw", [P, SEQ]), mt("z_silu", [P, SEQ])
        fq, fk, fv = mt("fq", [P, SEQ]), mt("fk", [P, TOK]), mt("fv", [P, TOK])
        sq, rs_t = mt("sq", [P, TOK]), mt("rs", [P, TOK])
        ln_t = sq
        q_dec = mt("q_dec", [P, SEQ])
        row = mt("row", [P, 3, TOK])
        g_exp, decay = mt("g_exp", [P, TOK]), mt("decay", [P, TOK])
        b_mat, qk, b_step = mt("b_mat", [P, TOK]), mt("qk", [P, TOK]), mt("b_step", [P, TOK])
        inv, inv_t, prod = mt("inv", [P, TOK]), mt("inv_t", [P, TOK]), mt("prod", [P, TOK])
        k_dec, k_dec_m = mt("k_dec", [P, 2, P]), mt("k_dec_m", [META, P])
        v_beta, v_beta_m = mt("v_beta", [P, 2, P]), mt("v_beta_m", [META, P])
        state, rhs, v_new = mt("state", [P, P]), mt("rhs", [P, P]), mt("v_new", [P, P])
        v_new_m = mt("v_new_m", [META, P])
        y_out = mt("y_out", [P, SEQ])
        f_bias, f_p = mt("f_bias", [P, META + P + TOK]), mt("f_p", [P, META + P + TOK])
        f_pt, f_pt_m = mt("f_pt", [P, 3 * P]), mt("f_pt_m", [META, SEQ])
        f_v, f_v_m = mt("f_v", [P, 2, P]), mt("f_v_m", [META, P])
        col = mt("col", [P, 3, 4])
        half_beta, neg_beta_eg, to_last, neg_g, eg_col = (mt(x, [P, 3]) for x in
                                                          ("half_beta", "neg_beta_eg", "to_last", "neg_g", "eg_col"))
        eg_last = mt("eg_last", [P, 2])
        f_max, f_sum, f_inv = mt("f_max", [P, 2]), mt("f_sum", [P, 2]), mt("f_inv", [P, 2])
        FW = (META + P, TOK)
        F_AT = (0, META + P)

        MB = 2 * MIX_TILES

        def norm_of_head(name, n):
            return n * 5 - 4 + ("gdn k", "gdn q", "fox q", "fox k", "gdn o").index(name)

        ORDER = {"k": 0, "v": 1, "q": 2, "z": 3, "fq": 4, "fk": 5, "fv": 6}

        GAP = 2
        SCHEDULE = ([(1, "start"), (16, "k"), (22, "q"), (26, "level", 0), (28, "fox q"), (32, "level", 1),
                     (36, "fox k"), (40, "level", 2), (44, "fox logits"), (48, "level", 3), (54, "fox out"),
                     (58, "level", 4), (64, "level", 5), (70, "level", 6), (76, "meta"), (82, "chunk", 0),
                     (92, "chunk", 1), (102, "out")])

        sc = Temps("scalars", [(ya_at + 16384, ya_at + 2 * KT * SEQ * 4)])
        sc_x, sc_xs, sc_out, sc_rate = (sc("x", [P, TOK]), sc("xs", [P, TOK]), sc("out", [P, TOK]),
                                        sc("rate", [P, 1]))
        sc_t = [sc(f"t{k}", [P, TOK]) for k in range(4)]

        gt = Temps("merge", [end_span])
        sig_a, sig_b, mix_a, mix_b, mix_v = (gt(x, [P, SEQ]) for x in ("sig_a", "sig_b", "mix_a", "mix_b", "mix_v"))
        ft = Temps("mlp", [mx_span])
        relu_t, hid_v = ft("relu", [P, 2, SEQ]), ft("hid", [P, 2, SEQ])
        at = Temps("att", [mx_span, (yb_at + KT * SEQ * 4, yb_at + 2 * KT * SEQ * 4), end_span])
        c_at = mx_at
        c_hi, c_lo = at("c_hi", [P, 2 * RT, SEQ], F32R), at("c_lo", [P, 2 * RT, SEQ], F32R)
        c_raw = at("c_raw", [P, 2 * RT, SEQ])
        pos_i = at("pos_i", [P, SEQ], I32)
        pos_f, angle, turns, reduced = (at(x, [P, SEQ]) for x in ("pos_f", "angle", "turns", "reduced"))
        cos_sin = {x: (at("cos_" + x, [P, SEQ]), at("sin_" + x, [P, SEQ])) for x in ("mla", "swa")}
        k_rope = at("k_rope", [P, SEQ])
        gate_s = at("gate_s", [P, 2, SEQ])
        gate_t = at("gate_t", [P, SEQ])
        q_m, k_m, v_m = (at(x, [P, 2, SEQ]) for x in ("q_m", "k_m", "v_m"))
        q_rope, rope_a, rope_b = (at(x, [P, SEQ]) for x in ("q_rope", "rope_a", "rope_b"))
        logits, probs, probs_t = (at(x, [P, 3 * P]) for x in ("logits", "probs", "probs_t"))
        row_max, row_sum, row_inv, row_sink = (at(x, [P, 2]) for x in ("row_max", "row_sum", "row_inv", "row_sink"))
        v_tok = at("v_tok", [P, 2, P])
        y_v = at("y_v", [P, SEQ])
        wt = Temps("swa", [(c_at, c_at + 6 * RT * SEQ * 4)])
        k_s = wt("k_s", [P, 4, SEQ])
        v_raw = wt("v_raw", [P, 2, SEQ])
        v_all = wt("v_all", [P, 2, 4, 64])
        k_own, v_own = wt("k_own", [P, SEQ]), wt("v_own", [P, 2, 64])
        sink, neg_sink = wt("sink", [P, 8]), wt("neg_sink", [P, 8])
        s_gate, s_th, s_y = (wt(x, [P, SEQ]) for x in ("gate", "th", "y"))
        q_s = wt("q_s", [P, SEQ])
        heads_before = {"mla": 0, "swa": HEADS}
        SWA_K_TURNS = 1 + HEADS // 2 + 1
        SWA_Q_TURNS = SWA_K_TURNS + 3
        W_AT, W_W = (0, P), (P, SEQ)

        block = ctx.enter_context(nc.Block())

        @block.sync
        def _(sp):
            for r in range(RING):
                sp.dma_start(raw[:, r], stream[r]).then_inc(landed[r], 16)
            with sp.Fori(1, STREAM // RING) as i:
                for r in range(RING):
                    sp.wait_ge(lo_ready, i * RING - RING + r + 1)
                    sp.dma_start(raw[:, r], stream[i * RING + r]).then_inc(landed[r], 16)
            sp.wait_ge(sem("norm done"), 6)
            sp.dma_start(out, h[:]).then_inc(sem("out written"), 16)
            sp.wait_ge(sem("out written"), 16)
            loads = STREAM // RING
            for r in range(RING):
                sp.wait_ge(landed[r], 16 * loads)

        @block.gpsimd
        def _(gp):
            gp.dma_start(consts[:], consts_in).then_inc(inputs_in, 16)
            gp.dma_start(vecs[:], vecs_in).then_inc(inputs_in, 16)
            gp.dma_start(xT[:], xT_in).then_inc(sem("x in"), 16)
            gp.wait_ge(sem("scalars"), 2)
            gp.dma_start(rows, sc_out[:]).then_inc(sem("rows out"), 16)
            gp.wait_ge(sem("rows out"), 16)
            by_head = rows.rearrange("(g r) n -> r g n", g=4)
            with gp.Fori(0, HEADS) as hd:
                gp.wait_ge(sem("row free"), hd + 1)
                gp.dma_start(row[:], by_head[bass.ts(hd, 1), 0:3, :].rearrange("a g n -> (a g) n")
                             .partition_broadcast(P)).then_inc(sem("row in"), 16)
            await_slab(gp, "out", -1)
            gp.dma_start(h[:], xT_in[:, :, META:]).then_inc(sem("h in"), 16)
            await_slab(gp, "mla_in", -1)
            gp.dma_start(pos_i[:], positions_in.partition_broadcast(P).rearrange("p a n -> p (a n)")).then_inc(
                sem("positions in"), 16)

        @block.tensor
        def _(pe):
            ident = const("identity", META, META + P)
            pe.sem_inc(slab_used, RING)
            for b in range(2):
                pe.sem_inc(tile_free[b], 1)
            pe.wait_ge(inputs_in, 32)
            norm_pe(pe, 0, TOK)
            pe.wait_ge(sem("norm lo"), KT)
            full_tile(pe, "scalars", 0, u_all, TOK, 0)
            pe.wait_ge(sem("scalars"), 2)
            for c, (t0, w) in enumerate(CHUNKS):
                mm = pe.transpose(bank[3][0:w, c * P:(c + 1) * P], sc_out[:, t0:t0 + w], ident)
            mm.then_inc(sem("scalar columns"), 1)

            def ones_sum(name, n, width):
                pe.wait_ge(sem("length sq"), norm_of_head(name, n))
                pe.matmul(bank[2][:, :width], const("ones"), sq[:, :width], start=True,
                          stop=True).then_inc(sem("length sum"), 1)

            def step_k(n):
                ones_sum("gdn k", n, TOK)
                yield
                pe.wait_ge(sem("unit"), n * 4 - 3)
                for c, (t0, w) in enumerate(CHUNKS):
                    o = bank[3][0:w, (c - 1) * P:c * P] if c else bank[3][0:w, 2 * P:3 * P]
                    mm = pe.transpose(o, kT[:, t0:t0 + w], ident)
                mm.then_inc(sem("k turned"), 1)
                for t0, w in MAIN_FIRST:
                    mm = pe.matmul(bank[5][0:w, t0:t0 + w], kT[:, t0:t0 + w], kT[:, t0:t0 + w], start=True,
                                   stop=True)
                mm.then_inc(sem("kk"), 1)
                for c, (t0, w) in enumerate(CHUNKS):
                    o = bank[4][0:w, (c - 1) * P:c * P] if c else bank[4][0:w, 2 * P:3 * P]
                    mm = pe.transpose(o, vT[:, t0:t0 + w], ident)
                mm.then_inc(sem("v turned"), 1)

            def step_q(n):
                ones_sum("gdn q", n, TOK)
                yield
                pe.wait_ge(sem("unit"), n * 4 - 2)
                for t0, w in MAIN:
                    mm = pe.matmul(bank[6][0:w, t0:t0 + w], kT[:, t0:t0 + w], qT[:, t0:t0 + w], start=True,
                                   stop=True)
                mm.then_inc(sem("qk"), 1)

            def step_level(n, lv):
                b = LEVELS[lv]
                spans = MAIN_FIRST if b < META else MAIN
                pe.wait_ge(sem("b step"), (n - 1) * len(LEVELS) + lv + 1)
                if lv:
                    pe.wait_ge(sem("inverse"), (n - 1) * 13 + 2 * lv)
                for t0, w in spans:
                    right = inv[0:w, t0:t0 + w] if lv else const("identity", t0, t0 + w, w)
                    mm = pe.matmul(bank[5][0:w, t0:t0 + w], b_step[0:w, t0:t0 + w], right, start=True, stop=True)
                mm.then_inc(sem("prod sum"), 1)
                if not lv:
                    return
                yield
                pe.wait_ge(sem("prod"), (n - 1) * 6 + lv)
                if b != LEVELS[-1]:
                    for t0, w in spans:
                        mm = pe.matmul(bank[6][0:w, t0:t0 + w], inv_t[0:w, t0:t0 + w], prod[0:w, t0:t0 + w],
                                       start=True, stop=True)
                    mm.then_inc(sem("step"), 1)
                for t0, w in spans:
                    mm = pe.matmul(bank[7][0:w, t0:t0 + w], prod[0:w, t0:t0 + w], inv_t[0:w, t0:t0 + w],
                                   start=True, stop=True)
                mm.then_inc(sem("step t"), 1)

            def step_meta(n):
                pe.wait_ge(sem("inverse"), (n - 1) * 13 + 13)
                pe.wait_ge(sem("v beta"), 3 * n)
                pe.wait_ge(sem("yb lo"), n)
                pe.matmul(bank[3][:, 0:P], inv_t[0:META, 0:P], v_beta_m[:, :], start=True,
                          stop=True).then_inc(sem("v new m sum"), 1)
                yield
                pe.wait_ge(sem("k dec"), 3 * n)
                pe.wait_ge(sem("v new m"), n)
                pe.matmul(bank[3][:, P:2 * P], k_dec_m[:, :], v_new_m[:, :], start=True,
                          stop=True).then_inc(sem("state sum"), 1)

            def step_chunk(n, c):
                t0, w = MAIN[c]
                o = bank[6][:, c * P:(c + 1) * P]
                pe.wait_ge(sem("state"), 2 * n - 1 + c)
                pe.matmul(bank[4][:, 0:P], kT[:, t0:t0 + w], state[:, :], start=True,
                          stop=True).then_inc(sem("k state"), 1)
                pe.wait_ge(sem("q dec"), n)
                pe.matmul(o, state[:, :], q_dec[:, c * P:(c + 1) * P], start=True, stop=False)
                yield
                pe.wait_ge(sem("rhs"), 2 * n - 1 + c)
                pe.matmul(bank[4][:, P:2 * P], inv_t[:, t0:t0 + w], rhs[:, :], start=True,
                          stop=True).then_inc(sem("v new sum"), 1)
                yield
                pe.wait_ge(sem("v new"), 2 * n - 1 + c)
                if c == 0:
                    pe.matmul(bank[3][:, P:2 * P], k_dec[:, 0], v_new[:, :], start=True,
                              stop=True).then_inc(sem("state sum"), 1)
                pe.matmul(o, v_new[:, :], qk[:, t0:t0 + w], start=False, stop=True).then_inc(sem("gdn o"), 1)

            def step_out(n):
                ones_sum("gdn o", n, SEQ)
                yield

            def step_fox_q(n):
                ones_sum("fox q", n, SEQ)
                yield

            def step_fox_k(n):
                ones_sum("fox k", n, TOK)
                pe.wait_ge(sem("k dec"), 3 * n)
                for c, (t0, w) in enumerate(CHUNKS):
                    o = bank[3][0:w, (c - 1) * P:c * P] if c else bank[3][0:w, 2 * P:3 * P]
                    mm = pe.transpose(o, fv[:, t0:t0 + w], ident)
                mm.then_inc(sem("fox v turned"), 1)
                yield

            def step_fox_logits(n):
                pe.wait_ge(sem("unit"), 4 * n)
                pe.wait_ge(sem("v beta"), 3 * n)
                for t in range(2):
                    mm = pe.matmul(bank[4][:, F_AT[t]:F_AT[t] + FW[t]], fq[:, t * P:(t + 1) * P],
                                   fk[:, 0:FW[t]], start=True, stop=True)
                mm.then_inc(sem("fox s"), 1)
                yield

            def step_fox_out(n):
                pe.wait_ge(sem("fox v"), 2 * n)
                pe.wait_ge(sem("fox p"), 2 * n)
                pe.transpose(bank[3][:, 0:P], f_p[:, META:META + P], ident)
                pe.transpose(bank[3][:, P:2 * P], f_p[:, F_AT[1] + META:F_AT[1] + META + P], ident)
                pe.transpose(bank[3][:, 2 * P:3 * P], f_p[:, F_AT[1] + META + P:F_AT[1] + TOK], ident)
                pe.transpose(bank[4][0:META, 0:P], f_p[:, 0:META], ident)
                pe.transpose(bank[4][0:META, P:2 * P], f_p[:, F_AT[1]:F_AT[1] + META],
                             ident).then_inc(sem("fox p turned"), 1)
                yield
                pe.wait_ge(sem("fox pt"), 2 * n)
                pe.matmul(bank[3][:, 0:SEQ], f_v_m[:, :], f_pt_m[:, :], start=True, stop=False)
                pe.matmul(bank[3][:, P:SEQ], f_v[:, 1], f_pt[:, SEQ:3 * P], start=False, stop=False,
                          skip_group_check=True)
                pe.matmul(bank[3][:, 0:SEQ], f_v[:, 0], f_pt[:, 0:SEQ], start=False,
                          stop=True).then_inc(sem("fox o"), 1)

            def mix_products(head, i=None):
                for j in range(MIX_TILES):
                    b, turn = tile_no("mix", head * MIX_TILES + j, i, 2 * MIX_TILES)
                    pe.wait_ge(tile_free[b], turn + 1)
                    x, w = (u_seq, SEQ) if j in (ORDER["z"], ORDER["fq"]) else (u_all, TOK)
                    o = proj[b][:, 0:w]
                    for half in range(2):
                        m, slot, _ = slab_no("mix", head * MB + 2 * j + half, i, 2 * MB)
                        pe.wait_ge(lo_ready, m + 1)
                        for k in range(HALF_KT):
                            w1, w2 = w_hi[:, slot, k * P:(k + 1) * P], w_lo[:, slot, k * P:(k + 1) * P]
                            x_hi, x_lo = x(half * HALF_KT + k)
                            pe.matmul(o, w1, x_hi, start=half == 0 and k == 0, stop=False)
                            pe.matmul(o, w1, x_lo, start=False, stop=False)
                            mm = pe.matmul(o, w2, x_hi, start=False, stop=half == 1 and k == HALF_KT - 1)
                            if k == HALF_KT - 1:
                                mm.then_inc(slab_used, 1)
                            yield

            steps_pe = {"k": step_k, "q": step_q, "level": step_level, "meta": step_meta, "chunk": step_chunk,
                        "out": step_out, "fox q": step_fox_q, "fox k": step_fox_k,
                        "fox logits": step_fox_logits, "fox out": step_fox_out}

            def mix(n, head, i=None):
                stream_ = mix_products(head, i) if head is not None else iter(())
                done = 0
                for at, name, *arg in SCHEDULE if n is not None else ():
                    for _ in range(max(0, at - done)):
                        next(stream_, None)
                    done = max(done, at)
                    if name in steps_pe:
                        for _ in steps_pe[name](n, *arg):
                            for _ in range(GAP):
                                next(stream_, None)
                            done += GAP
                for _ in stream_:
                    pass

            mix(None, 0)
            with pe.Fori(0, HEADS // 2 - 1) as i:
                mix(i * 2 + 1, 1, i)
                mix(i * 2 + 2, 2, i)
            mix(HEADS - 1, HEADS - 1)
            mix(HEADS, None)
            pe.wait_ge(sem("ya lo"), HEADS)
            pe.wait_ge(sem("yb lo"), HEADS)
            with pe.Fori(0, KT) as i:
                for j, x in enumerate((u_seq, u_seq, ya, yb)):
                    full_tile(pe, "merge", j, x, SEQ, 2 * j, i, 8, 4)

            def matrix(phase, x):
                with pe.Fori(0, KT // 2) as i:
                    for s in range(2):
                        full_tile(pe, phase, s, x, SEQ, 2 * s, i, 4, 2)

            pe.wait_ge(sem("mix lo"), KT)
            matrix("out", mx)
            norm_pe(pe, 1, SEQ)
            pe.wait_ge(sem("norm lo"), 2 * KT)
            for q in range(QUARTERS):
                matrix(f"up{q}", u_seq)
                pe.wait_ge(sem("hidden lo"), (q + 1) * KT)
                matrix(f"down{q}", ya)
            norm_pe(pe, 2, SEQ)
            norm_pe(pe, 3, SEQ)
            pe.wait_ge(sem("norm lo"), 3 * KT)
            for t in range(MLA_IN_TILES):
                full_tile(pe, "mla_in", t, u_seq, SEQ, 2 * t)
            for g in range(2):
                for k in range(RT):
                    pe.wait_ge(sem("c sq"), g * RT + k + 1)
                    pe.matmul(bank[2][:, :SEQ], const("ones"), norm_sq[:, k, :SEQ], start=k == 0,
                              stop=k == RT - 1).then_inc(sem("c sum"), 1)
            pe.matmul(bank[6][:, :SEQ], const("turn_mla"), k_rope[:], start=True, stop=True).then_inc(
                sem("turned half"), 1)

            def softmax_pe(tag, c, scores, value, o):
                c = heads_before[tag] + c
                scores()
                pe.wait_ge(sem("head p"), 2 * c)
                pe.transpose(bank[3][:, 0:P], probs[:, 0:P], ident)
                pe.transpose(bank[3][:, P:2 * P], probs[:, P:2 * P], ident)
                pe.transpose(bank[3][:, 2 * P:3 * P], probs[:, 2 * P:3 * P], ident).then_inc(
                    sem("head p turned"), 1)
                pe.wait_ge(sem("head pt"), c)
                pe.matmul(o[:, 0:P], value(0), probs_t[:, 0:P], start=True, stop=True)
                pe.matmul(o[:, P:SEQ], value(0), probs_t[:, P:2 * P], start=True, stop=False)
                pe.matmul(o[:, P:SEQ], value(1), probs_t[:, 2 * P:3 * P], start=False, stop=True).then_inc(
                    sem("head o"), 1)

            pe.wait_ge(sem("c lo"), 2 * RT)
            pe.wait_ge(sem("rotated"), 1)
            with pe.Fori(0, HEADS // 2) as i:
                for s in range(2):
                    full_tile(pe, "mla", s, u_seq, SEQ, 2 * s, i, 8, 8)

                def small_tile(slab, s, o, x0):
                    _, slot, _ = slab_no("mla", slab, i, 8)
                    for k in range(RT):
                        e = (s * RT + k) * P
                        pe.matmul(o, w_hi[:, slot, e:e + P], c_hi[:, x0 + k], start=k == 0, stop=False)
                        pe.matmul(o, w_hi[:, slot, e:e + P], c_lo[:, x0 + k], start=False, stop=False)
                        mm = pe.matmul(o, w_lo[:, slot, e:e + P], c_hi[:, x0 + k], start=False,
                                       stop=k == RT - 1)
                    return mm

                for j in range(3):
                    pe.wait_ge(lo_ready, slab_no("mla", 4 + j, i, 8)[0] + 1)
                    for s in range(2):
                        b, turn = tile_no("mla", 2 + 2 * j + s, i, 8)
                        pe.wait_ge(tile_free[b], turn + 1)
                        small_tile(4 + j, s, proj[b][:, 0:SEQ], 0 if j == 0 else RT).then_inc(
                            slab_used if s else sem("mla first half"), 1)
                pe.wait_ge(lo_ready, slab_no("mla", 7, i, 8)[0] + 1)
                pe.wait_ge(sem("mla qr free"), i + 1)
                small_tile(7, 0, bank[7][:, 0:SEQ], 0).then_inc(slab_used, 1)
                pe.wait_ge(sem("mla qr"), i + 1)
                pe.matmul(bank[6][:, :SEQ], const("turn_mla"), q_rope[:], start=True, stop=True).then_inc(
                    sem("turned half"), 1)
                for s in range(2):
                    c = i * 2 + s + 1

                    def scores():
                        if s == 0:
                            pe.wait_ge(sem("rotated"), i + 2)
                        r = slice(64 * s, 64 * s + 64)
                        for t in range(2):
                            o = bank[2][:, W_AT[t]:W_AT[t] + W_W[t]]
                            pe.matmul(o, q_m[:, s, t * P:(t + 1) * P], k_m[:, s, 0:W_W[t]], start=True, stop=False)
                            mm = pe.matmul(o, q_rope[r, t * P:(t + 1) * P], k_rope[r, 0:W_W[t]], start=False,
                                           stop=True)
                        mm.then_inc(sem("head s"), 1)
                        for t in range(2):
                            mm = pe.transpose(bank[4][:, t * P:(t + 1) * P], v_m[:, s, t * P:(t + 1) * P], ident)
                        mm.then_inc(sem("mla v turned"), 1)
                        pe.wait_ge(sem("mla v"), c)

                    softmax_pe("mla", c, scores, lambda t: v_tok[:, t], bank[5])
            pe.wait_ge(sem("mla lo"), HEADS)
            matrix("mla_out", ya)
            norm_pe(pe, 4, SEQ)
            pe.wait_ge(sem("norm lo"), 4 * KT)
            for t in range(SWA_KV_TILES):
                full_tile(pe, "swa_kv", t, u_seq, SEQ, 2 * t)
            for t in range(SWA_KV_TILES):
                b, turn = tile_no("swa_kv", t)
                pe.wait_ge(tile_free[b], turn + 2)
            for t in range(4):
                if t:
                    pe.wait_ge(sem("rotated"), t + SWA_K_TURNS - 1)
                pe.matmul(bank[6][:, :SEQ], const("turn_swa"), k_s[:, t], start=True, stop=True).then_inc(
                    sem("turned half"), 1)
            for t in range(2):
                for m in range(2):
                    mm = pe.transpose(bank[4][:, (2 * t + m) * P:(2 * t + m + 1) * P],
                                      v_raw[:, m, t * P:(t + 1) * P], ident)
            mm.then_inc(sem("swa v turned"), 1)
            with pe.Fori(0, 4) as i:
                for j in range(4):
                    full_tile(pe, "swa", 2 * j, u_seq, SEQ, 4 * j, i, 16, 8)
                    full_tile(pe, "swa", 2 * j + 1, u_seq, SEQ, 4 * j + 2, i, 16, 8)
                    n = i * 4 + j + 1
                    b, turn = tile_no("swa", 2 * j, i, 8)
                    pe.wait_ge(tile_free[b], turn + 2)
                    pe.matmul(bank[6][:, :SEQ], const("turn_swa"), q_s[:], start=True, stop=True).then_inc(
                        sem("turned half"), 1)
                    for s in range(2):
                        c = i * 8 + j * 2 + s + 1

                        def scores():
                            r = slice(64 * s, 64 * s + 64)
                            if s == 0:
                                pe.wait_ge(sem("rotated"), n + SWA_Q_TURNS)
                            for t in range(2):
                                mm = pe.matmul(bank[2][:, W_AT[t]:W_AT[t] + W_W[t]], q_s[r, t * P:(t + 1) * P],
                                               k_own[r, 0:W_W[t]], start=True, stop=True)
                            mm.then_inc(sem("head s"), 1)

                        softmax_pe("swa", c, scores, lambda t: v_own[:, t], bank[5][64 * s:64 * s + 64])
            pe.wait_ge(sem("swa lo"), KT)
            matrix("swa_out", ya)
            norm_pe(pe, 5, SEQ)

        @block.scalar
        def _(act):
            act.wait_ge(inputs_in, 32)
            act.wait_ge(sem("x in"), 16)
            act.preload_act_table_set("natural_log_exp_and_others")
            norm_act(act, 0, xT, TOK, 0)
            split_hi(act, "scalars", 0)
            split_hi(act, "scalars", 1)
            split_hi(act, "scalars", 2)
            split_hi(act, "scalars", 3)
            act.wait_ge(sem("sc dve"), 1)
            act.activation(sc_t[0][:], sc_xs[:], ACT.Abs).then_inc(sem("sc act"), 1)
            act.wait_ge(sem("sc act"), 1)
            act.activation(sc_t[1][:], sc_t[0][:], ACT.Exp, scale=-1.0).then_inc(sem("sc act"), 1)
            act.activation(sc_rate[:], vec("a_log"), ACT.Exp).then_inc(sem("sc act"), 1)
            act.wait_ge(sem("sc act"), 2)
            act.activation(sc_t[2][:], sc_t[1][:], ACT.Ln, bias=1.0).then_inc(sem("sc act"), 1)
            act.activation(sc_t[3][:], sc_x[:], ACT.Tanh, scale=0.5).then_inc(sem("sc act"), 1)
            for c, (t0, w) in enumerate(CHUNKS):
                act.wait_ge(sem("scalar columns"), 1)
                act.activation(tokcol[0:w, c], bank[3][0:w, c * P:(c + 1) * P].rearrange(
                    "p (g r) -> p g r", g=4), ACT.Copy).then_inc(sem("tokcol"), 1)

            def rsqrt(name, n, src, width, pre, scale):
                at_ = norm_of_head(name, n)
                act.activation(sq[:, :width], src, ACT.Square, scale=pre).then_inc(sem("length sq"), 1)
                act.wait_ge(sem("length sum"), at_)
                act.activation(ln_t[:, :width], bank[2][:, :width], ACT.Ln, scale=scale,
                               bias=const("eps")).then_inc(sem("length ln"), 1)
                act.wait_ge(sem("length ln"), at_)
                act.activation(rs_t[:, :width], ln_t[:, :width], ACT.Exp, scale=-0.5).then_inc(
                    sem("length rs"), 1)

            def step_start(n):
                for c, y in enumerate((kT, vT, qT)):
                    act.wait_ge(sem("conv"), n * 12 - 8 + 4 * c)
                    if c:
                        act.wait_ge(sem("silu"), n * 4 - 4 + c)
                    act.activation(gate_th[:], y[:], ACT.Tanh, scale=0.5).then_inc(sem("silu tanh"), 1)
                act.wait_ge(sem("silu"), n * 4 - 1)
                act.activation(gate_th[:, :SEQ], z_raw[:], ACT.Tanh, scale=0.5).then_inc(sem("silu tanh"), 1)
                act.preload_act_table_set("natural_log_exp_and_others")

            def step_k(n):
                rsqrt("gdn k", n, kT[:], TOK, 0.5, 1.0)
                act.wait_ge(sem("col"), n)
                act.wait_ge(sem("row in"), n * 16)
                act.activation(half_beta[:], col[:, :, 0], ACT.Copy, scale=0.5).then_inc(sem("cols"), 1)
                act.activation(neg_g[:], col[:, :, 1], ACT.Copy, scale=-1.0).then_inc(sem("cols"), 1)
                act.activation(eg_col[:], col[:, :, 1], ACT.Exp).then_inc(sem("cols"), 1)
                for c, (t0, w) in enumerate(CHUNKS):
                    act.activation(to_last[:, c:c + 1], col[:, c, 1:2], ACT.Exp, scale=-1.0,
                                   bias=row[:, 1, t0 + w - 1:t0 + w]).then_inc(sem("cols"), 1)
                act.activation(eg_last[:, 0:1], row[:, 1, META + P - 1:META + P],
                               ACT.Exp).then_inc(sem("cols"), 1)
                act.wait_ge(sem("cols"), 7 * n)
                act.wait_ge(sem("g diff"), n)
                for c, (t0, w) in enumerate(CHUNKS):
                    act.activation(decay[:, t0:t0 + w], b_step[:, t0:t0 + w], ACT.Exp,
                                   bias=neg_g[:, c:c + 1]).then_inc(sem("decay"), 1)

            def step_q(n):
                act.wait_ge(sem("silu"), n * 4 - 1)
                act.wait_ge(sem("unit"), n * 4 - 3)
                rsqrt("gdn q", n, qT[:], TOK, 0.5, 1.0)
                act.activation(g_exp[:], row[:, 1], ACT.Exp).then_inc(sem("g exp"), 1)
                act.wait_ge(sem("k turned"), n)
                act.activation(k_dec_m[:, :], bank[3][0:META, 2 * P:3 * P], ACT.Copy,
                               scale=to_last[0:META, 0:1]).then_inc(sem("k dec"), 1)
                for c in range(2):
                    act.activation(k_dec[:, c], bank[3][:, c * P:(c + 1) * P], ACT.Copy,
                                   scale=to_last[:, c + 1:c + 2]).then_inc(sem("k dec"), 1)
                act.wait_ge(sem("v turned"), n)
                act.activation(v_beta_m[:, :], bank[4][0:META, 2 * P:3 * P], ACT.Copy,
                               scale=half_beta[0:META, 0:1]).then_inc(sem("v beta"), 1)
                for c in range(2):
                    act.activation(v_beta[:, c], bank[4][:, c * P:(c + 1) * P], ACT.Copy,
                                   scale=half_beta[:, c + 1:c + 2]).then_inc(sem("v beta"), 1)

            def step_level(n, lv):
                if not lv:
                    return
                act.wait_ge(sem("prod sum"), (n - 1) * 7 + lv + 1)
                lo = 0 if LEVELS[lv] < META else META
                act.activation(prod[:, lo:], bank[5][:, lo:TOK], ACT.Copy).then_inc(sem("prod"), 1)

            def step_meta(n):
                act.wait_ge(sem("v new m sum"), n)
                act.activation(v_new_m[:, :], bank[3][0:META, 0:P], ACT.Copy).then_inc(sem("v new m"), 1)
                act.wait_ge(sem("state sum"), 2 * n - 1)
                act.activation(state[:], bank[3][:, P:2 * P], ACT.Copy).then_inc(sem("state"), 1)

            def step_chunk(n, c):
                act.wait_ge(sem("v new sum"), 2 * n - 1 + c)
                act.activation(v_new[:], bank[4][:, P:2 * P], ACT.Copy).then_inc(sem("v new"), 1)

            def step_out(n):
                act.wait_ge(sem("gdn o"), 2 * n)
                act.wait_ge(sem("unit"), 4 * n)
                rsqrt("gdn o", n, bank[6][:, 0:SEQ], SEQ, 1.0, 1.0 / P)
                act.wait_ge(sem("gdn y"), 2 * n)
                act.activation(ya_hi[:, bass.ts(n - 1, 1), :], y_out[:, None, :], ACT.Copy).then_inc(
                    sem("ya hi"), 1)

            def step_fox_q(n):
                act.wait_ge(sem("unit"), n * 4 - 2)
                rsqrt("fox q", n, fq[:], SEQ, 1.0, 1.0 / P)

            def step_fox_k(n):
                act.wait_ge(sem("unit"), n * 4 - 1)
                rsqrt("fox k", n, fk[:], TOK, 1.0, 1.0 / P)
                act.wait_ge(sem("fox v turned"), n)
                act.activation(f_v[:], bank[3][:, 0:2 * P].rearrange("p (c d) -> p c d", c=2),
                               ACT.Copy).then_inc(sem("fox v"), 1)
                act.activation(f_v_m[:, :], bank[3][0:META, 2 * P:3 * P], ACT.Copy).then_inc(sem("fox v"), 1)

            def step_fox_logits(n):
                act.wait_ge(sem("fox max"), 2 * n)
                for t in range(2):
                    w = slice(F_AT[t], F_AT[t] + FW[t])
                    act.activation(f_p[:, w], f_bias[:, w], ACT.Exp, bias=f_max[:, t:t + 1],
                                   accum_out=f_sum[:, t:t + 1]).then_inc(sem("fox e"), 1)

            def step_fox_out(n):
                act.wait_ge(sem("fox p turned"), n)
                act.activation(f_pt[:], bank[3][:, 0:3 * P], ACT.Copy).then_inc(sem("fox pt"), 1)
                act.activation(f_pt_m[:, :], bank[4][0:META, 0:SEQ], ACT.Copy).then_inc(sem("fox pt"), 1)
                act.wait_ge(sem("fox o"), n)
                act.activation(yb_hi[:, bass.ts(n - 1, 1), :], bank[3][:, None, 0:SEQ],
                               ACT.Copy).then_inc(sem("yb hi"), 1)

            dest = [conv_in[0], conv_in[1], conv_in[2], z_raw, fq, fk, fv]

            def mix_stream(head, i, upto, done):
                for k in range(done, upto):
                    if k % HALF_KT == 0 and k < MIX_TILES * KT:
                        split_hi(act, "mix", head * MB + k // HALF_KT + 2, i, 2 * MB)
                    if k % KT == 1 and k > 1:
                        j = k // KT - 1
                        await_slab(act, "mix", head * MB + 2 * j + 1, i, 2 * MB)
                        b, _ = tile_no("mix", head * MIX_TILES + j)
                        w = SEQ if j in (ORDER["z"], ORDER["fq"]) else TOK
                        o = dest[j][:, 3:] if j < 3 else dest[j][:]
                        act.activation(o, proj[b][:, 0:w], ACT.Copy).then_inc(tile_free[b], 1)

            steps_act = {"start": step_start, "k": step_k, "q": step_q, "level": step_level, "meta": step_meta,
                         "chunk": step_chunk, "out": step_out, "fox q": step_fox_q, "fox k": step_fox_k,
                         "fox logits": step_fox_logits, "fox out": step_fox_out}

            def mix(n, head, i=None):
                done = 0
                for at, name, *arg in SCHEDULE if n is not None else ():
                    if head is not None:
                        mix_stream(head, i, at, done)
                        done = max(at, done)
                    steps_act[name](n, *arg)
                if head is not None:
                    mix_stream(head, i, MIX_TILES * KT + 2, done)

            mix(None, 0)
            with act.Fori(0, HEADS // 2 - 1) as i:
                mix(i * 2 + 1, 1, i)
                mix(i * 2 + 2, 2, i)
            mix(HEADS - 1, HEADS - 1)
            mix(HEADS, None)

            def ahead(phase, n, i=None, per=0):
                split_hi(act, phase, n, i, per)
                split_hi(act, phase, n + 1, i, per)

            with act.Fori(0, KT) as i:
                for j in range(MERGE_TILES):
                    ahead("merge", 2 * j + 2, i, 8)
                    if j < 2:
                        await_slab(act, "merge", 2 * j + 1, i, 8)
                        b, _ = tile_no("merge", j)
                        act.activation((sig_a, sig_b)[j][:], proj[b][:, 0:SEQ], ACT.Tanh,
                                       scale=0.5).then_inc(tile_free[b], 1)
                act.wait_ge(sem("mix v"), i + 1)
                act.activation(mx_hi[:, bass.ts(i, 1), :], mix_v[:, None, :], ACT.Copy,
                               scale=0.5).then_inc(sem("mix hi"), 1)

            def matrix(phase):
                with act.Fori(0, KT // 2) as i:
                    for s in range(2):
                        ahead(phase, 2 * s + 2, i, 4)

            matrix("out")
            act.preload_act_table_set("natural_log_exp_and_others")
            await_tiles_out(act, "up0")
            norm_act(act, 1, h, SEQ, 1)
            for q in range(QUARTERS):
                with act.Fori(0, KT // 2) as i:
                    for s in range(2):
                        ahead(f"up{q}", 2 * s + 2, i, 4)
                        await_slab(act, f"up{q}", 2 * s + 1, i, 4)
                        b, _ = tile_no(f"up{q}", s)
                        act.activation(relu_t[:, s], proj[b][:, 0:SEQ], ACT.Relu).then_inc(tile_free[b], 1)
                        act.wait_ge(sem("hidden v"), i * 2 + (q * KT + s + 1))
                        act.activation(ya_hi[:, bass.ts(i * 2 + s, 1), :], hid_v[:, s, None, :],
                                       ACT.Copy).then_inc(sem("hidden hi"), 1)
                matrix(f"down{q}")
            await_tiles_out(act, "mla_in")
            norm_act(act, 2, h, SEQ, None)
            norm_act(act, 3, h, SEQ, 2)
            for t in range(MLA_IN_TILES):
                ahead("mla_in", 2 * t + 2)
                await_slab(act, "mla_in", 2 * t + 1)
                b, _ = tile_no("mla_in", t)
                act.activation(c_raw[:, t] if t < 2 * RT else k_rope[:], proj[b][:, 0:SEQ],
                               ACT.Copy).then_inc(tile_free[b], 1)
            await_tiles_out(act, "mla")
            for g in range(2):
                for k in range(RT):
                    if g:
                        act.wait_ge(sem("c sum"), k + 1)
                    act.activation(norm_sq[:, k, :SEQ], c_raw[:, g * RT + k], ACT.Square).then_inc(sem("c sq"), 1)
                if g:
                    act.wait_ge(sem("c v"), RT)
                act.wait_ge(sem("c sum"), (g + 1) * RT)
                act.activation(norm_ln[:, :SEQ], bank[2][:, :SEQ], ACT.Ln, scale=1.0 / MLA_RANK,
                               bias=const("eps")).then_inc(sem("c ln"), 1)
                act.wait_ge(sem("c ln"), g + 1)
                act.activation(norm_rs[:, :SEQ], norm_ln[:, :SEQ], ACT.Exp, scale=-0.5).then_inc(sem("c rs"), 1)
                for k in range(RT):
                    act.wait_ge(sem("c v"), g * RT + k + 1)
                    act.activation(c_hi[:, g * RT + k], c_raw[:, g * RT + k], ACT.Copy).then_inc(sem("c hi"), 1)
            for n in range(4):
                act.wait_ge(sem("angle reduced"), n + 1)
                act.activation(cos_sin[("mla", "swa")[n // 2]][1 - n % 2][:], reduced[:],
                               ACT.Sin).then_inc(sem("trig"), 1)

            def softmax_act(tag, c, sinks=None):
                max_at = 2 * c if sinks is None else 2 * HEADS + c
                c = heads_before[tag] + c
                act.wait_ge(sem("head max"), max_at)
                for t in range(2):
                    w = slice(W_AT[t], W_AT[t] + W_W[t])
                    act.activation(probs[:, w], logits[:, w], ACT.Exp, bias=row_max[:, t:t + 1],
                                   accum_out=row_sum[:, t:t + 1]).then_inc(sem("head e"), 1)
                if sinks is not None:
                    act.activation(row_sink[:], row_max[:], ACT.Exp, bias=sinks).then_inc(sem("head e"), 1)
                act.wait_ge(sem("head p turned"), c)
                act.activation(probs_t[:], bank[3][:, 0:3 * P], ACT.Copy).then_inc(sem("head pt"), 1)

            with act.Fori(0, HEADS // 2) as i:
                for s in range(2):
                    ahead("mla", 2 * s + 2, i, 8)
                    await_slab(act, "mla", 2 * s + 1, i, 8)
                    if s:
                        b, turn = tile_no("mla", 0, i, 8)
                        act.wait_ge(tile_free[b], turn + 2)
                    b, _ = tile_no("mla", s)
                    act.activation(gate_t[:], proj[b][:, 0:SEQ], ACT.Tanh, scale=0.5).then_inc(
                        sem("mla tanh"), 1)
                for j, dst in enumerate((q_m, k_m, v_m)):
                    split_hi(act, "mla", 6 + j, i, 8)
                    for s in range(2):
                        if s:
                            await_slab(act, "mla", 4 + j, i, 8)
                        else:
                            act.wait_ge(sem("mla first half"), i * 3 + j + 1)
                        b, _ = tile_no("mla", 2 + 2 * j + s)
                        act.activation(dst[:, s], proj[b][:, 0:SEQ], ACT.Copy).then_inc(tile_free[b], 1)
                split_hi(act, "mla", 9, i, 8)
                await_slab(act, "mla", 7, i, 8)
                act.activation(q_rope[:], bank[7][:, 0:SEQ], ACT.Copy).then_inc(sem("mla qr"), 1)
                for s in range(2):
                    c = i * 2 + s + 1
                    act.wait_ge(sem("mla v turned"), c)
                    act.activation(v_tok[:], bank[4][:, 0:SEQ].rearrange("p (t d) -> p t d", t=2),
                                   ACT.Copy).then_inc(sem("mla v"), 1)
                    softmax_act("mla", c)
                    act.wait_ge(sem("mla y"), c)
                    act.activation(ya_hi[:, bass.ts(i * 2 + s, 1), :], y_v[:, None, :], ACT.Copy).then_inc(
                        sem("mla hi"), 1)
            matrix("mla_out")
            await_tiles_out(act, "swa_kv")
            act.preload_act_table_set("natural_log_exp_and_others")
            norm_act(act, 4, h, SEQ, 3)
            for t in range(SWA_KV_TILES):
                ahead("swa_kv", 2 * t + 2)
                await_slab(act, "swa_kv", 2 * t + 1)
                b, _ = tile_no("swa_kv", t)
                act.activation(k_s[:, t] if t < 4 else v_raw[:, t - 4], proj[b][:, 0:SEQ],
                               ACT.Copy).then_inc(tile_free[b], 1)
            act.wait_ge(sem("swa v turned"), 1)
            act.activation(v_all[:].rearrange("p t g d -> p (t g d)"), bank[4][:, :],
                           ACT.Copy).then_inc(sem("swa v"), 1)
            with act.Fori(0, 4) as i:
                for j in range(4):
                    n = i * 4 + j + 1
                    ahead("swa", 4 * j + 2, i, 16)
                    await_slab(act, "swa", 4 * j + 1, i, 16)
                    b, _ = tile_no("swa", 2 * j)
                    act.activation(q_s[:], proj[b][:, 0:SEQ], ACT.Copy).then_inc(tile_free[b], 1)
                    ahead("swa", 4 * j + 4, i, 16)
                    await_slab(act, "swa", 4 * j + 3, i, 16)
                    b, _ = tile_no("swa", 2 * j + 1)
                    act.activation(s_th[:], proj[b][:, 0:SEQ], ACT.Tanh, scale=0.5).then_inc(
                        sem("swa tanh"), 1)
                    for s in range(2):
                        softmax_act("swa", i * 8 + j * 2 + s + 1, sink[:, 2 * j + s:2 * j + s + 1])
                    act.wait_ge(sem("swa y"), n)
                    act.activation(ya_hi[:, bass.ts(i * 4 + j, 1), :], s_y[:, None, :], ACT.Copy).then_inc(
                        sem("swa hi"), 1)
            matrix("swa_out")
            act.preload_act_table_set("natural_log_exp_and_others")
            await_tiles_out(act, "end")
            norm_act(act, 5, h, SEQ, None)

        @block.vector
        def _(dve):
            dve.wait_ge(inputs_in, 32)
            dve.memset(tokcol[:], 0.0).then_inc(sem("cleared"), 1)
            for b in (5, 6, 7):
                dve.memset(bank[b][:, 0:META], 0.0).then_inc(sem("cleared"), 1)
            dve.wait_ge(sem("x in"), 16)
            norm_dve(dve, 0, xT, TOK, "mix_norm", 0)
            split_lo(dve, "scalars", 0)
            split_lo(dve, "scalars", 1)
            for x in range(3):
                dve.memset(conv_in[x][:, 0:3], 0.0).then_inc(sem("cleared"), 1)
            split_lo(dve, "scalars", 2)
            split_lo(dve, "scalars", 3)
            await_slab(dve, "scalars", 1)
            b, _ = tile_no("scalars", 0)
            dve.tensor_scalar(sc_x[:], proj[b][:, 0:TOK], vec("bias"), None, ALU.add).then_inc(tile_free[b], 1)
            dve.wait_ge(tile_free[b], 2)
            dve.tensor_scalar(sc_xs[:], sc_x[:], const("sign"), None, ALU.mult).then_inc(sem("sc dve"), 1)
            dve.wait_ge(sem("sc act"), 4)
            dve.scalar_tensor_tensor(out=sc_t[0][:], in0=sc_xs[:], scalar=0.0, in1=sc_t[2][:], op0=ALU.max,
                                     op1=ALU.add).then_inc(sem("sc dve"), 1)
            dve.wait_ge(sem("sc dve"), 2)
            dve.wait_ge(sem("sc act"), 4)
            dve.tensor_scalar(sc_t[1][:], sc_t[0][:], sc_rate[:, 0:1], -1.0, ALU.mult,
                              ALU.mult).then_inc(sem("sc dve"), 1)
            dve.wait_ge(sem("sc dve"), 3)
            dve.tensor_tensor_scan(sc_out[:], const("reset"), sc_t[1][:], 0.0, ALU.mult,
                                   ALU.add).then_inc(sem("scalars"), 1)
            dve.wait_ge(sem("scalars"), 1)
            dve.wait_ge(sem("sc act"), 5)
            dve.tensor_scalar(sc_out[0:HEADS, :], sc_t[3][0:HEADS, :], 0.5, 0.5, ALU.mult,
                              ALU.add).then_inc(sem("scalars"), 1)
            dve.sem_inc(sem("row free"), 1)
            dve.wait_ge(sem("tokcol"), 3)

            conv_w = vecs[:, VEC_AT["conv"][0]:VEC_AT["conv"][1]].rearrange("p (t k) -> p t k", k=4)

            def step_start(n):
                for c, y in enumerate((kT, vT, qT)):
                    tile0 = (HEADS, 2 * HEADS, 0)[c]
                    for tap in (3, 2, 1, 0):
                        w_tap = conv_w[:, bass.ts(n - 1 + tile0, 1), tap]
                        src = conv_in[c][:, tap:tap + TOK]
                        if tap == 3:
                            dve.tensor_scalar(y[:], src, w_tap, None, ALU.mult).then_inc(sem("conv"), 1)
                        else:
                            dve.wait_ge(sem("conv"), n * 12 - 9 + 4 * c - tap)
                            dve.scalar_tensor_tensor(out=y[:], in0=src, scalar=w_tap, in1=y[:], op0=ALU.mult,
                                                     op1=ALU.add).then_inc(sem("conv"), 1)
                    if c:
                        silu(n, c - 1)
                silu(n, 2)
                dve.tensor_copy(col[:], tokcol[:, :, :, bass.ts(n - 1, 1)].rearrange(
                    "p c g r -> p c (g r)")).then_inc(sem("col"), 1)
                dve.wait_ge(sem("row in"), n * 16)
                dve.tensor_tensor(b_step[:], row[:, 1], const("future"), ALU.add).then_inc(sem("g diff"), 1)
                dve.wait_ge(sem("silu tanh"), n * 4)
                dve.scalar_tensor_tensor(out=z_silu[:], in0=gate_th[:, :SEQ], scalar=1.0, in1=z_raw[:],
                                         op0=ALU.add, op1=ALU.mult).then_inc(sem("silu"), 1)

            def silu(n, c):
                y = (kT, vT, qT)[c]
                dve.wait_ge(sem("silu tanh"), n * 4 - 3 + c)
                dve.scalar_tensor_tensor(out=y[:], in0=gate_th[:], scalar=1.0, in1=y[:], op0=ALU.add,
                                         op1=ALU.mult).then_inc(sem("silu"), 1)

            def unit(name, n, y, width, scalar):
                dve.wait_ge(sem("length rs"), norm_of_head(name, n))
                dve.scalar_tensor_tensor(out=y[:, :width], in0=y[:, :width], scalar=scalar,
                                         in1=rs_t[:, :width], op0=ALU.mult, op1=ALU.mult).then_inc(sem("unit"), 1)

            def step_k(n):
                unit("gdn k", n, kT, TOK, 0.5)
                dve.wait_ge(sem("col"), n)
                for t in range(2):
                    dve.scalar_tensor_tensor(out=f_bias[:, F_AT[t]:F_AT[t] + FW[t]], in0=row[:, 2, 0:FW[t]],
                                             scalar=col[:, t + 1, 2:3], in1=const(f"fox{t}"), op0=ALU.subtract,
                                             op1=ALU.subtract, reverse1=True).then_inc(sem("fox bias"), 1)
                dve.wait_ge(sem("decay"), 3 * n)
                dve.wait_ge(sem("kk"), n)
                dve.tensor_tensor(b_mat[:], bank[5][:, 0:TOK], decay[:], ALU.mult).then_inc(sem("b mat"), 1)
                dve.wait_ge(sem("b mat"), 2 * n - 1)
                dve.tensor_tensor(b_mat[:], b_mat[:], row[:, 0], ALU.mult).then_inc(sem("b mat"), 1)
                dve.wait_ge(sem("b mat"), 2 * n)
                blocks_of(n, 0)
                dve.wait_ge(sem("b step"), n * 7 - 6)
                dve.tensor_tensor(inv_t[:], const("identity"), b_step[:], ALU.subtract).then_inc(
                    sem("inverse"), 1)

            def blocks_of(n, lv):
                lo = 0 if LEVELS[lv] < META else META
                dve.tensor_tensor(b_step[:, lo:], b_mat[:, lo:], const(f"level{LEVELS[lv]}", lo),
                                  ALU.mult).then_inc(sem("b step"), 1)

            def step_q(n):
                unit("gdn q", n, qT, TOK, 0.5 * HEAD_SCALE)
                dve.wait_ge(sem("cols"), 7 * n)
                dve.scalar_tensor_tensor(out=neg_beta_eg[:], in0=col[:, :, 0], scalar=-1.0, in1=eg_col[:],
                                         op0=ALU.mult, op1=ALU.mult).then_inc(sem("neg beta eg"), 1)
                dve.wait_ge(sem("unit"), n * 4 - 2)
                dve.wait_ge(sem("g exp"), n)
                dve.tensor_tensor(q_dec[:], qT[:, META:], g_exp[:, META:], ALU.mult).then_inc(sem("q dec"), 1)
                dve.wait_ge(sem("qk"), n)
                dve.tensor_tensor(qk[:, META:], bank[6][:, META:TOK], decay[:, META:],
                                  ALU.mult).then_inc(sem("qk decayed"), 1)
                dve.wait_ge(sem("fox bias"), 2 * n)
                dve.sem_inc(sem("row free"), 1)

            def step_level(n, lv):
                lo = 0 if LEVELS[lv] < META else META
                dve.wait_ge(sem("prod sum"), (n - 1) * 7 + lv + 1)
                if not lv:
                    blocks_of(n, 1)
                    dve.tensor_tensor(inv[:], const("identity"), bank[5][:, 0:TOK],
                                      ALU.subtract).then_inc(sem("inverse"), 1)
                    return
                if lv + 1 < len(LEVELS):
                    blocks_of(n, lv + 1)
                    dve.wait_ge(sem("step"), (n - 1) * 5 + lv)
                    dve.tensor_tensor(inv[:, lo:], inv[:, lo:], bank[6][:, lo:TOK],
                                      ALU.subtract).then_inc(sem("inverse"), 1)
                dve.wait_ge(sem("step t"), (n - 1) * 6 + lv)
                dve.tensor_tensor(inv_t[:, lo:], inv_t[:, lo:], bank[7][:, lo:TOK],
                                  ALU.subtract).then_inc(sem("inverse"), 1)

            def step_meta(n):
                pass

            def step_chunk(n, c):
                dve.wait_ge(sem("neg beta eg"), n)
                dve.wait_ge(sem("v beta"), 3 * n)
                dve.wait_ge(sem("k state"), 2 * n - 1 + c)
                dve.scalar_tensor_tensor(out=rhs[:], in0=bank[4][:, 0:P], scalar=neg_beta_eg[:, c + 1:c + 2],
                                         in1=v_beta[:, c], op0=ALU.mult, op1=ALU.add).then_inc(sem("rhs"), 1)
                if c == 0:
                    dve.wait_ge(sem("state sum"), 2 * n)
                    dve.wait_ge(sem("state"), 2 * n - 1)
                    dve.scalar_tensor_tensor(out=state[:], in0=state[:], scalar=eg_last[:, 0:1],
                                             in1=bank[3][:, P:2 * P], op0=ALU.mult,
                                             op1=ALU.add).then_inc(sem("state"), 1)

            def step_out(n):
                dve.wait_ge(sem("length rs"), norm_of_head("gdn o", n))
                dve.scalar_tensor_tensor(out=y_out[:], in0=bank[6][:, 0:SEQ], scalar=vec("gdn_norm"),
                                         in1=rs_t[:, :SEQ], op0=ALU.mult, op1=ALU.mult).then_inc(
                                             sem("gdn y"), 1)
                dve.wait_ge(sem("gdn y"), 2 * n - 1)
                dve.wait_ge(sem("silu"), n * 4)
                dve.scalar_tensor_tensor(out=y_out[:], in0=y_out[:], scalar=0.5, in1=z_silu[:], op0=ALU.mult,
                                         op1=ALU.mult).then_inc(sem("gdn y"), 1)
                dve.wait_ge(sem("ya hi"), n)
                dve.tensor_tensor(ya_lo[:, bass.ts(n - 1, 1), :], y_out[:, None, :],
                                  ya_hi[:, bass.ts(n - 1, 1), :].bitcast(F32), ALU.subtract).then_inc(
                                      sem("ya lo"), 1)

            def step_fox_q(n):
                unit("fox q", n, fq, SEQ, vec("fox_q"))

            def step_fox_k(n):
                unit("fox k", n, fk, TOK, vec("fox_k"))

            def step_fox_logits(n):
                dve.wait_ge(sem("fox s"), n)
                dve.scalar_tensor_tensor(out=f_bias[:], in0=bank[4][:, 0:F_AT[1] + FW[1]], scalar=HEAD_SCALE,
                                         in1=f_bias[:], op0=ALU.mult, op1=ALU.add).then_inc(
                                             sem("fox logits"), 1)
                dve.wait_ge(sem("fox logits"), n)
                for t in range(2):
                    dve.tensor_reduce(f_max[:, t:t + 1], f_bias[:, F_AT[t]:F_AT[t] + FW[t]], AX.X, ALU.max,
                                      negate=True).then_inc(sem("fox max"), 1)
                dve.wait_ge(sem("fox e"), 2 * n)
                dve.reciprocal(f_inv[:], f_sum[:]).then_inc(sem("fox inv"), 1)
                dve.wait_ge(sem("fox inv"), n)
                for t in range(2):
                    o = f_p[:, F_AT[t]:F_AT[t] + FW[t]]
                    dve.tensor_scalar(o, o, f_inv[:, t:t + 1], None, ALU.mult).then_inc(sem("fox p"), 1)

            def step_fox_out(n):
                dve.wait_ge(sem("yb hi"), n)
                dve.tensor_tensor(yb_lo[:, bass.ts(n - 1, 1), :], bank[3][:, None, 0:SEQ],
                                  yb_hi[:, bass.ts(n - 1, 1), :].bitcast(F32), ALU.subtract).then_inc(
                                      sem("yb lo"), 1)

            steps_dve = {"start": step_start, "k": step_k, "q": step_q, "level": step_level, "meta": step_meta,
                         "chunk": step_chunk, "out": step_out, "fox q": step_fox_q, "fox k": step_fox_k,
                         "fox logits": step_fox_logits, "fox out": step_fox_out}

            def mix_stream(head, i, upto, done):
                for k in range(done, upto):
                    if k % HALF_KT == 0 and k < MIX_TILES * KT:
                        split_lo(dve, "mix", head * MB + k // HALF_KT + 2, i, 2 * MB)

            def mix(n, head, i=None):
                done = 0
                if n is not None:
                    for j in range(2):
                        b, turn = tile_no("mix", (head if head is not None else HEADS) * MIX_TILES - 1 - j, i,
                                          2 * MIX_TILES)
                        dve.wait_ge(tile_free[b], turn + 2)
                for at, name, *arg in SCHEDULE if n is not None else ():
                    if head is not None:
                        mix_stream(head, i, at, done)
                        done = max(at, done)
                    steps_dve[name](n, *arg)
                if head is not None:
                    mix_stream(head, i, MIX_TILES * KT, done)

            mix(None, 0)
            with dve.Fori(0, HEADS // 2 - 1) as i:
                mix(i * 2 + 1, 1, i)
                mix(i * 2 + 2, 2, i)
            mix(HEADS - 1, HEADS - 1)
            mix(HEADS, None)

            def ahead(phase, n, i=None, per=0):
                split_lo(dve, phase, n, i, per)
                split_lo(dve, phase, n + 1, i, per)

            def await_tile_out(phase, n, i=None, per=0):
                b, turn = tile_no(phase, n, i, per)
                dve.wait_ge(tile_free[b], turn + 2)

            with dve.Fori(0, KT) as i:
                for j in range(MERGE_TILES):
                    ahead("merge", 2 * j + 2, i, 8)
                    if j >= 2:
                        if j == 2:
                            await_tile_out("merge", 0, i, 4)
                            await_tile_out("merge", 1, i, 4)
                        await_slab(dve, "merge", 2 * j + 1, i, 8)
                        b, _ = tile_no("merge", j)
                        dve.scalar_tensor_tensor(out=(mix_a, mix_b)[j - 2][:], in0=(sig_a, sig_b)[j - 2][:],
                                                 scalar=1.0, in1=proj[b][:, 0:SEQ], op0=ALU.add,
                                                 op1=ALU.mult).then_inc(tile_free[b], 1)
                await_tile_out("merge", 2, i, 4)
                await_tile_out("merge", 3, i, 4)
                dve.tensor_tensor(mix_v[:], mix_a[:], mix_b[:], ALU.add).then_inc(sem("mix v"), 1)
                dve.wait_ge(sem("mix hi"), i + 1)
                dve.scalar_tensor_tensor(out=mx_lo[:, bass.ts(i, 1), :], in0=mix_v[:, None, :], scalar=0.5,
                                         in1=mx_hi[:, bass.ts(i, 1), :].bitcast(F32), op0=ALU.mult,
                                         op1=ALU.subtract).then_inc(sem("mix lo"), 1)

            def residual(phase):
                with dve.Fori(0, KT // 2) as i:
                    for s in range(2):
                        ahead(phase, 2 * s + 2, i, 4)
                        await_slab(dve, phase, 2 * s + 1, i, 4)
                        b, _ = tile_no(phase, s)
                        o = h[:, bass.ts(i * 2 + s, 1), :]
                        dve.tensor_tensor(o, proj[b][:, None, 0:SEQ], o, ALU.add).then_inc(tile_free[b], 1)

            dve.wait_ge(sem("h in"), 16)
            residual("out")
            norm_dve(dve, 1, h, SEQ, "mlp_norm", 1)
            for q in range(QUARTERS):
                with dve.Fori(0, KT // 2) as i:
                    for s in range(2):
                        ahead(f"up{q}", 2 * s + 2, i, 4)
                        await_tile_out(f"up{q}", s, i, 2)
                        dve.tensor_tensor(hid_v[:, s], relu_t[:, s], relu_t[:, s], ALU.mult).then_inc(
                            sem("hidden v"), 1)
                        dve.wait_ge(sem("hidden hi"), i * 2 + (q * KT + s + 1))
                        t = bass.ts(i * 2 + s, 1)
                        dve.tensor_tensor(ya_lo[:, t, :], hid_v[:, s, None, :], ya_hi[:, t, :].bitcast(F32),
                                          ALU.subtract).then_inc(sem("hidden lo"), 1)
                residual(f"down{q}")
            norm_dve(dve, 2, h, SEQ, "final_norm", None)
            norm_dve(dve, 3, h, SEQ, "layer0", 2)
            for t in range(MLA_IN_TILES):
                ahead("mla_in", 2 * t + 2)
            for g in range(2):
                dve.wait_ge(sem("c rs"), g + 1)
                for k in range(RT):
                    o = c_raw[:, g * RT + k]
                    dve.scalar_tensor_tensor(out=o, in0=o, scalar=vec(("mla_q", "mla_kv")[g], k),
                                             in1=norm_rs[:, :SEQ], op0=ALU.mult, op1=ALU.mult).then_inc(
                                                 sem("c v"), 1)
                for k in range(RT):
                    dve.wait_ge(sem("c hi"), g * RT + k + 1)
                    dve.tensor_tensor(c_lo[:, g * RT + k], c_raw[:, g * RT + k],
                                      c_hi[:, g * RT + k].bitcast(F32), ALU.subtract).then_inc(sem("c lo"), 1)

            steps = [0]

            def step(ins):
                steps[0] += 1
                ins.then_inc(sem("angle step"), 1)
                dve.wait_ge(sem("angle step"), steps[0])

            dve.wait_ge(sem("positions in"), 16)
            step(dve.tensor_copy(pos_f[:], pos_i[:]))
            for n in range(4):
                shift = n % 2
                if n % 2 == 0:
                    step(dve.tensor_scalar(angle[:], pos_f[:], const("freq_" + ("mla", "swa")[n // 2]), None,
                                           ALU.mult))
                step(dve.tensor_scalar(turns[:], angle[:], float(1 / (2 * np.pi)), 0.25 * shift, ALU.mult,
                                       ALU.add))
                step(dve.tensor_scalar(turns[:], turns[:], ROUND, None, ALU.add))
                step(dve.tensor_scalar(turns[:], turns[:], ROUND, None, ALU.subtract))
                if n:
                    dve.wait_ge(sem("trig"), n)
                step(dve.scalar_tensor_tensor(out=reduced[:], in0=turns[:], scalar=-TURN_HI, in1=angle[:],
                                              op0=ALU.mult, op1=ALU.add))
                step(dve.scalar_tensor_tensor(out=reduced[:], in0=turns[:], scalar=-TURN_LO, in1=reduced[:],
                                              op0=ALU.mult, op1=ALU.add))
                step(dve.tensor_scalar(reduced[:], reduced[:], float(np.pi / 2 * shift), None, ALU.add))
                dve.tensor_scalar(reduced[:], reduced[:], PI_BELOW, -PI_BELOW, ALU.min, ALU.max).then_inc(
                    sem("angle reduced"), 1)

            def rope(n, x, kind):
                cos, sin = cos_sin[kind]
                dve.wait_ge(sem("turned half"), n)
                dve.tensor_tensor(rope_a[:], x, cos[:], ALU.mult).then_inc(sem("rotation parts"), 1)
                dve.tensor_tensor(rope_b[:], bank[6][:, 0:SEQ], sin[:], ALU.mult).then_inc(sem("rotation parts"), 1)
                dve.wait_ge(sem("rotation parts"), 2 * n)
                dve.tensor_tensor(x, rope_a[:], rope_b[:], ALU.add).then_inc(sem("rotated"), 1)

            dve.wait_ge(sem("trig"), 4)
            rope(1, k_rope[:], "mla")

            def softmax_dve(tag, c, scale, mask, sinks=None):
                e_at = 2 * c if sinks is None else 2 * HEADS + 3 * c
                key_max_at = 2 * c
                c = heads_before[tag] + c
                dve.wait_ge(sem("head s"), c)
                dve.scalar_tensor_tensor(out=logits[:], in0=bank[2][:, 0:3 * P], scalar=scale, in1=const(mask),
                                         op0=ALU.mult, op1=ALU.add).then_inc(sem("head logits"), 1)
                dve.wait_ge(sem("head logits"), c)
                top_ = sem("head max" if sinks is None else "head key max")
                for t in range(2):
                    dve.tensor_reduce(row_max[:, t:t + 1], logits[:, W_AT[t]:W_AT[t] + W_W[t]], AX.X, ALU.max,
                                      negate=True).then_inc(top_, 1)
                if sinks is None:
                    dve.wait_ge(sem("head e"), e_at)
                else:
                    dve.wait_ge(top_, key_max_at)
                    dve.tensor_scalar(row_max[:], row_max[:], sinks, None, ALU.min).then_inc(sem("head max"), 1)
                    dve.wait_ge(sem("head e"), e_at)
                    dve.tensor_tensor(row_sum[:], row_sum[:], row_sink[:], ALU.add).then_inc(
                        sem("head sum"), 1)
                    dve.wait_ge(sem("head sum"), c - HEADS)
                dve.reciprocal(row_inv[:], row_sum[:]).then_inc(sem("head inv"), 1)
                dve.wait_ge(sem("head inv"), c)
                for t in range(2):
                    o = probs[:, W_AT[t]:W_AT[t] + W_W[t]]
                    dve.tensor_scalar(o, o, row_inv[:, t:t + 1], None, ALU.mult).then_inc(sem("head p"), 1)

            dve.sem_inc(sem("mla qr free"), 1)
            with dve.Fori(0, HEADS // 2) as i:
                for s in range(2):
                    ahead("mla", 2 * s + 2, i, 8)
                    dve.wait_ge(sem("mla tanh"), i * 2 + s + 1)
                    b, _ = tile_no("mla", s)
                    dve.scalar_tensor_tensor(out=gate_s[:, s], in0=gate_t[:], scalar=1.0, in1=proj[b][:, 0:SEQ],
                                             op0=ALU.add, op1=ALU.mult).then_inc(tile_free[b], 1)
                for j in range(3):
                    split_lo(dve, "mla", 6 + j, i, 8)
                split_lo(dve, "mla", 9, i, 8)
                rope(i + 2, q_rope[:], "mla")
                dve.sem_inc(sem("mla qr free"), 1)
                for s in range(2):
                    c = i * 2 + s + 1
                    softmax_dve("mla", c, MLA_SCALE, "causal")
                    dve.wait_ge(sem("head o"), c)
                    if s == 0:
                        await_tile_out("mla", 0, i, 8)
                        await_tile_out("mla", 1, i, 8)
                    dve.scalar_tensor_tensor(out=y_v[:], in0=bank[5][:, 0:SEQ], scalar=0.5, in1=gate_s[:, s],
                                             op0=ALU.mult, op1=ALU.mult).then_inc(sem("mla y"), 1)
                    dve.wait_ge(sem("mla hi"), c)
                    t = bass.ts(i * 2 + s, 1)
                    dve.tensor_tensor(ya_lo[:, t, :], y_v[:, None, :], ya_hi[:, t, :].bitcast(F32),
                                      ALU.subtract).then_inc(sem("mla lo"), 1)
            residual("mla_out")
            norm_dve(dve, 4, h, SEQ, "layer1", 3)
            for t in range(SWA_KV_TILES):
                ahead("swa_kv", 2 * t + 2)
            for t in range(4):
                rope(t + SWA_K_TURNS, k_s[:, t], "swa")
            dve.wait_ge(sem("rotated"), SWA_K_TURNS + 3)
            dve.wait_ge(sem("swa v"), 1)
            sink_at = VEC_AT["sinks"][0]
            with dve.Fori(0, 4) as i:
                dve.tensor_copy(k_own[:, None, :], k_s[:, bass.ts(i, 1), :]).then_inc(sem("swa own"), 1)
                dve.tensor_copy(v_own[:, :, None, :], v_all[:, :, bass.ts(i, 1), :]).then_inc(sem("swa own"), 1)
                dve.tensor_copy(sink[:], vecs[:, bass.ds(i * 8 + sink_at, 8)]).then_inc(sem("swa own"), 1)
                dve.tensor_scalar(neg_sink[:], vecs[:, bass.ds(i * 8 + sink_at, 8)], -1.0, None,
                                  ALU.mult).then_inc(sem("swa own"), 1)
                dve.wait_ge(sem("swa own"), i * 4 + 4)
                for j in range(4):
                    n = i * 4 + j + 1
                    ahead("swa", 4 * j + 2, i, 16)
                    ahead("swa", 4 * j + 4, i, 16)
                    dve.wait_ge(sem("swa tanh"), n)
                    b, _ = tile_no("swa", 2 * j + 1)
                    dve.scalar_tensor_tensor(out=s_gate[:], in0=s_th[:], scalar=1.0, in1=proj[b][:, 0:SEQ],
                                             op0=ALU.add, op1=ALU.mult).then_inc(tile_free[b], 1)
                    rope(n + SWA_Q_TURNS, q_s[:], "swa")
                    for s in range(2):
                        softmax_dve("swa", i * 8 + j * 2 + s + 1, SWA_SCALE, "window",
                                    neg_sink[:, 2 * j + s:2 * j + s + 1])
                    dve.wait_ge(sem("head o"), 2 * n + HEADS)
                    await_tile_out("swa", 2 * j + 1, i, 8)
                    dve.scalar_tensor_tensor(out=s_y[:], in0=bank[5][:, 0:SEQ], scalar=0.5, in1=s_gate[:],
                                             op0=ALU.mult, op1=ALU.mult).then_inc(sem("swa y"), 1)
                    dve.wait_ge(sem("swa hi"), n)
                    t = bass.ts(i * 4 + j, 1)
                    dve.tensor_tensor(ya_lo[:, t, :], s_y[:, None, :], ya_hi[:, t, :].bitcast(F32),
                                      ALU.subtract).then_inc(sem("swa lo"), 1)
            residual("swa_out")
            norm_dve(dve, 5, h, SEQ, "final2", None)


def slabs_of(w):
    k, n = w.shape
    return w.reshape(k // (HALF_KT * P), HALF_KT, P, n // P, P).transpose(3, 0, 2, 1, 4)


def lay_out(i):
    f32 = np.float32
    stream = np.zeros((STREAM, P, HALF_KT, P), f32)
    pos = [0]

    def put(slabs):
        slabs = slabs.reshape(-1, P, HALF_KT, P)
        stream[pos[0]:pos[0] + len(slabs)] = slabs
        pos[0] += len(slabs)

    w_in = np.asarray(i["w_in"])[0]
    edges = np.cumsum([0, 6144, 2048, 16, 16, 6144, 16, 2048, 2048])
    qkv_a, z_a, b_a, a_a, qkv_b, f_b, gate_a, gate_b = (w_in[:, a:b] for a, b in zip(edges[:-1], edges[1:]))
    scalars = np.zeros((D, P), f32)
    scalars[:, 0:16], scalars[:, 32:48], scalars[:, 64:80] = b_a, a_a, f_b
    put(slabs_of(scalars))
    qa, ka, va = (slabs_of(qkv_a[:, j * D:(j + 1) * D]) for j in range(3))
    qb, kb, vb = (slabs_of(qkv_b[:, j * D:(j + 1) * D]) for j in range(3))
    put(np.stack([ka, va, qa, slabs_of(z_a), qb, kb, vb], axis=1))
    put(np.stack([slabs_of(gate_a), slabs_of(gate_b), slabs_of(np.asarray(i["w_o_gdn"])[0]),
                  slabs_of(np.asarray(i["w_o_fox"])[0])], axis=1))
    put(slabs_of(np.asarray(i["w_out"])[0]))
    up, down = np.asarray(i["w_up"])[0], np.asarray(i["w_down"])[0]
    for q in range(QUARTERS):
        put(slabs_of(up[:, q * D:(q + 1) * D]))
        put(slabs_of(down[q * D:(q + 1) * D]))
    mla = np.asarray(i["mla_w_in_2"])[0]
    c_q, c_kv, k_r, gate = (mla[:, a:b] for a, b in ((0, 512), (512, 1024), (1024, 1088), (1088, 3136)))
    put(slabs_of(np.concatenate([c_q, c_kv, k_r, k_r], axis=1)))

    def quarters(w):
        return w.reshape(RT, P, -1, P).transpose(2, 1, 0, 3)

    uq = np.asarray(i["mla_w_uq_2"])[0].reshape(MLA_RANK, HEADS, 192)
    ukv = np.asarray(i["mla_w_ukv_2"])[0].reshape(MLA_RANK, HEADS, 256)
    qn = quarters(uq[:, :, :P].reshape(MLA_RANK, -1))
    qr = quarters(uq[:, :, P:].reshape(MLA_RANK, -1))
    kn = quarters(ukv[:, :, :P].reshape(MLA_RANK, -1))
    vv = quarters(ukv[:, :, P:].reshape(MLA_RANK, -1))
    gates = slabs_of(gate)
    for pair in range(HEADS // 2):
        a, b = 2 * pair, 2 * pair + 1
        put(gates[a:b + 1])
        for x in (qn, kn, vv):
            put(np.concatenate([x[a], x[b]], axis=1))
        put(np.concatenate([qr[pair], np.zeros_like(qr[pair])], axis=1))
    put(slabs_of(np.asarray(i["mla_w_out_2"])[0]))
    swa = np.asarray(i["swa_w_in_2"])[0]
    q, k, v, gate = (swa[:, a:b] for a, b in ((0, 2048), (2048, 2304), (2304, 2560), (2560, 4608)))
    k = k.reshape(D, 4, 64)
    put(slabs_of(np.concatenate([k, k], axis=2).reshape(D, 512)))
    put(slabs_of(v))
    put(np.stack([slabs_of(q), slabs_of(gate)], axis=1))
    put(slabs_of(np.asarray(i["swa_w_out_2"])[0]))

    vecs = np.zeros((P, VEC_N), f32)

    def vec(name, a):
        lo, hi = VEC_AT[name]
        vecs[:a.shape[0], lo:hi] = a

    def column(a):
        return np.asarray(a).reshape(-1, P).T

    vec("mix_norm", column(i["mix_norm_g"]))
    vec("mlp_norm", column(i["mlp_norm_g"]))
    vec("final_norm", column(i["final_norm_g"]))
    vec("layer0", column(i["layer_norm_2"][0]))
    vec("layer1", column(i["layer_norm_2"][1]))
    vec("final2", column(i["final_norm_2"]))
    vec("conv", np.asarray(i["conv_w"])[0].reshape(4, 48, P).transpose(2, 1, 0).reshape(P, -1))
    vec("gdn_norm", column(i["gdn_norm_g"]))
    vec("fox_q", column(i["fox_q_norm_g"]))
    vec("fox_k", column(i["fox_k_norm_g"]))
    bias, a_log = np.zeros((P, 1), f32), np.zeros((P, 1), f32)
    bias[32:48, 0], bias[64:80, 0] = np.asarray(i["dt_bias"])[0], np.asarray(i["fox_f_bias"])[0]
    a_log[32:48, 0] = np.asarray(i["a_log"])[0]
    vec("bias", bias)
    vec("a_log", a_log)
    vec("mla_q", column(i["mla_q_norm_2"]))
    vec("mla_kv", column(i["mla_kv_norm_2"]))
    vec("sinks", np.broadcast_to(np.asarray(i["swa_sinks_2"])[0], (P, 32)))
    x = np.concatenate([np.asarray(i["meta_tokens"]), np.asarray(i["x"])[0]], axis=0)
    xT = x.T.reshape(KT, P, TOK).transpose(1, 0, 2)
    return {"stream": stream.reshape(STREAM, P, SLAB), "consts": CONST, "vecs": vecs,
            "xT": np.ascontiguousarray(xT), "positions": np.asarray(i["positions_2"])}


def kernel(**inputs):
    import concourse.bacc as bacc
    from concourse.bass_utils import run_bass_kernel_spmd

    nc = bacc.Bacc("TRN2", target_bir_lowering=False, num_devices=1)
    arrays = lay_out(inputs)
    args = {k: nc.dram_tensor(f"in_{k}", a.shape, mybir.dt.from_np(a.dtype), kind="ExternalInput").ap()
            for k, a in arrays.items()}
    rows = nc.dram_tensor("rows", (P, TOK), F32, kind="Internal").ap()
    out = nc.dram_tensor("out_dram", (P, KT, SEQ), F32, kind="ExternalOutput").ap()
    program(nc, args["stream"], args["consts"], args["vecs"], args["xT"], args["positions"], rows, out)
    r = run_bass_kernel_spmd(nc, [{f"in_{k}": a for k, a in arrays.items()}], core_ids=[0])
    y = r.results[0]["out_dram"]
    return np.ascontiguousarray(y.transpose(1, 0, 2).reshape(1, D, SEQ).transpose(0, 2, 1))
```
